# Optimizing a Trainium2 kernel written in Bass

```python
import math
import jax, jax.numpy as jnp
from jax import lax
import numpy as np

D_MODEL = 1024
BATCH = 1
SEQ = 128
DEPTH = 1
DEC_BATCH = 1
DEC_SEQ = 512
PAST_LEN = 128

GRID_W = 64
D_MIX = D_MODEL
D_RWKV = D_MIX // 2
D_HYENA = D_MIX - D_RWKV
RWKV_HEAD = 64
RWKV_HEADS = D_RWKV // RWKV_HEAD
DECAY_LORA = 64
ICLR_LORA = 64
GATE_LORA = 128
HYENA_ORDER = 2
FILTER_BANDS = 8
FILTER_EMB = 1 + 2 * FILTER_BANDS
FILTER_HIDDEN = 64
DECAY_TARGET = 1e-2
FAST_DECAY_PCT = 0.3
SLOW_DECAY_PCT = 1.5
N_KEYS = 128
N_EXPERTS = N_KEYS * N_KEYS
PEER_HEADS = 8
PEER_TOPK = 16
PEER_DKEY = 256
PEER_HALF = PEER_DKEY // 2
PEER_CHUNK = 128
D_IN = 3 * D_RWKV + 3 * D_HYENA
EPS = 1e-6
GN_EPS = 64e-5

kernel_name = 'hymba_rwkv7_hyena_peer_diffusion_step'

def rmsnorm(x, g):
    xf = x.astype(jnp.float32)
    y = xf * lax.rsqrt(jnp.mean(xf * xf, axis=-1, keepdims=True) + EPS)
    return (y * g.astype(jnp.float32)).astype(x.dtype)

def short_conv(u, w, grid_w):
    B, L, C = u.shape
    if grid_w is not None:
        rows = L // grid_w
        u = u.reshape(B * rows, grid_w, C)
    up = jnp.pad(u, ((0, 0), (1, 1), (0, 0)))
    y = up[:, :-2] * w[0] + up[:, 1:-1] * w[1] + up[:, 2:] * w[2]
    return y.reshape(B, L, C)

def wkv_scan(s0, r, dec, k, v, kk, kka, reverse):
    def step(s, inp):
        r_t, d_t, k_t, v_t, kk_t, kka_t = inp
        sa = jnp.einsum('bhij,bhj->bhi', s, kk_t)
        s = s * d_t[:, :, None, :] - sa[..., None] * kka_t[:, :, None, :] + v_t[..., None] * k_t[:, :, None, :]
        y = jnp.einsum('bhij,bhj->bhi', s, r_t)
        return s, y
    xs = tuple(jnp.moveaxis(a, 1, 0) for a in (r, dec, k, v, kk, kka))
    s_fin, ys = lax.scan(step, s0, xs, reverse=reverse)
    return s_fin, jnp.moveaxis(ys, 0, 1)

def rwkv_mix(h, r, k, v, s0, p, l):
    B, L, _ = h.shape
    def heads(t):
        return t.astype(jnp.float32).reshape(B, L, RWKV_HEADS, RWKV_HEAD)
    g = jax.nn.sigmoid(h @ p['rwkv_g1'][l]) @ p['rwkv_g2'][l]
    kk = heads(k * p['rwkv_k_k'][l])
    kk = kk * lax.rsqrt(jnp.maximum(jnp.sum(kk * kk, -1, keepdims=True), 1e-24))
    rh = heads(r)
    vh = heads(v)
    y_sum = jnp.zeros_like(rh)
    bonus = jnp.zeros_like(rh)
    finals = []
    for d in range(2):
        w = p['rwkv_w0'][l, d] + jnp.tanh(h @ p['rwkv_w1'][l, d]) @ p['rwkv_w2'][l, d]
        dec = jnp.exp(-jnp.exp(-jax.nn.softplus(-w.astype(jnp.float32)) - 0.5))
        a = jax.nn.sigmoid(p['rwkv_a0'][l, d] + (h @ p['rwkv_a1'][l, d]) @ p['rwkv_a2'][l, d])
        kd = heads(k * (1 + (a - 1) * p['rwkv_k_a'][l]))
        s_fin, y = wkv_scan(s0[:, d].astype(jnp.float32), rh, heads(dec), kd, vh, kk, kk * heads(a), reverse=(d == 1))
        y_sum = y_sum + y
        bonus = bonus + jnp.sum(rh * kd * p['rwkv_r_k'][l, d].astype(jnp.float32), -1, keepdims=True) * vh
        finals.append(s_fin)
    mu = jnp.mean(y_sum, -1, keepdims=True)
    var = jnp.mean(jnp.square(y_sum - mu), -1, keepdims=True)
    yn = ((y_sum - mu) * lax.rsqrt(var + GN_EPS)).reshape(B, L, D_RWKV)
    yn = yn * p['rwkv_ln_w'][l] + p['rwkv_ln_b'][l]
    out = (yn + bonus.reshape(B, L, D_RWKV)) * g
    return out.astype(h.dtype), jnp.stack(finals, axis=1)

def hyena_filters(L, p, l):
    t = jnp.linspace(0.0, 1.0, L, dtype=jnp.float32)[:, None]
    wpos = 2.0 * math.pi * jnp.arange(L, dtype=jnp.float32)[:, None] / L
    f = jnp.linspace(1e-4, FILTER_BANDS - 1, FILTER_BANDS, dtype=jnp.float32)[None, :]
    z = jnp.concatenate([t, jnp.cos(f * wpos), -jnp.sin(f * wpos)], axis=-1)
    hid = jnp.sin(p['hy_freq'][l, 0] * (z @ p['hy_f_w1'][l] + p['hy_f_b1'][l]))
    hid = jnp.sin(p['hy_freq'][l, 1] * (hid @ p['hy_f_w2'][l] + p['hy_f_b2'][l]))
    filt = (hid @ p['hy_f_w3'][l]).astype(jnp.float32).reshape(L, 2 * HYENA_ORDER, D_HYENA)
    max_decay = math.log(DECAY_TARGET) / FAST_DECAY_PCT
    min_decay = math.log(DECAY_TARGET) / SLOW_DECAY_PCT
    deltas = jnp.linspace(min_decay, max_decay, D_HYENA, dtype=jnp.float32)
    window = jnp.exp(-t * jnp.abs(deltas))
    return filt * window[:, None, :]

def fft_causal(u, filt):
    L = u.shape[1]
    n = 2 * L
    uf = jnp.fft.rfft(u, n=n, axis=1)
    hf = jnp.fft.rfft(filt, n=n, axis=0)
    return jnp.fft.irfft(uf * hf[None], n=n, axis=1)[:, :L]

def bidir_long_conv(u, h_fwd, h_bwd, bias):
    y = fft_causal(u, h_fwd) + jnp.flip(fft_causal(jnp.flip(u, 1), h_bwd), 1)
    return y + u * bias

def hyena_mix(v, x1, x2, p, l):
    L = v.shape[1]
    filt = hyena_filters(L, p, l)
    bias = p['hy_bias'][l].astype(jnp.float32)
    z = x1.astype(jnp.float32) * bidir_long_conv(v.astype(jnp.float32), filt[:, 0], filt[:, 1], bias[0])
    z = x2.astype(jnp.float32) * bidir_long_conv(z, filt[:, 2], filt[:, 3], bias[1])
    return rmsnorm(z, p['hy_norm'][l]).astype(v.dtype)

def mixer(h, s0, grid_w, p, l):
    u = short_conv(h @ p['w_in'][l], p['conv_w'][l], grid_w)
    cuts = [D_RWKV, 2 * D_RWKV, 3 * D_RWKV, 3 * D_RWKV + D_HYENA, 3 * D_RWKV + 2 * D_HYENA]
    r, k, v, hv, hx1, hx2 = jnp.split(u, cuts, axis=-1)
    ya, s_fin = rwkv_mix(h, r, k, v, s0, p, l)
    yb = hyena_mix(hv, hx1, hx2, p, l)
    return jnp.concatenate([ya, yb], axis=-1) @ p['w_out'][l], s_fin

def peer(h, p, l):
    B, L, D = h.shape
    T = B * L
    x = h.reshape(T, D)
    q = (x @ p['peer_wq'][l]).reshape(T, PEER_HEADS, 2, PEER_HALF)
    s = jnp.einsum('thpd,phkd->thpk', q, p['peer_keys'][l])
    sv, si = lax.top_k(s, PEER_TOPK)
    cand = sv[:, :, 0, :, None] + sv[:, :, 1, None, :]
    cidx = si[:, :, 0, :, None] * N_KEYS + si[:, :, 1, None, :]
    top_s, pos = lax.top_k(cand.reshape(T, PEER_HEADS, PEER_TOPK * PEER_TOPK), PEER_TOPK)
    eidx = jnp.take_along_axis(cidx.reshape(T, PEER_HEADS, PEER_TOPK * PEER_TOPK), pos, axis=-1)
    gate = jax.nn.softmax(top_s.astype(jnp.float32), axis=-1).astype(h.dtype)
    u_tab = p['peer_u'][l]
    v_tab = p['peer_v'][l]
    nc = T // PEER_CHUNK
    def chunk(args):
        xc, ic, gc = args
        act = jax.nn.gelu(jnp.einsum('cd,ced->ce', xc, u_tab[ic]), approximate=False) * gc
        return jnp.einsum('ce,ced->cd', act, v_tab[ic])
    out = lax.map(chunk, (x.reshape(nc, PEER_CHUNK, D),
                          eidx.reshape(nc, PEER_CHUNK, PEER_HEADS * PEER_TOPK),
                          gate.reshape(nc, PEER_CHUNK, PEER_HEADS * PEER_TOPK)))
    return out.reshape(B, L, D)

def layer(x, mod, s0, grid_w, p, l):
    shift1, scale1, gate1, shift2, scale2, gate2 = jnp.split(mod, 6, axis=-1)
    h = rmsnorm(x, p['norm_mix'][l]) * (1 + scale1) + shift1
    m, s_fin = mixer(h, s0, grid_w, p, l)
    x = x + gate1 * m
    h = rmsnorm(x, p['norm_ffn'][l]) * (1 + scale2) + shift2
    x = x + gate2 * peer(h, p, l)
    return x, s_fin

def setup_inputs(seed: int = 0) -> dict:
    key = jax.random.key(seed)
    ks = iter(jax.random.split(key, 64))
    def nrm(shape, scale):
        return scale * jax.random.normal(next(ks), shape, jnp.float32)
    def gain(shape):
        return 1.0 + nrm(shape, 0.05)
    return {
        'x_prompt': nrm((BATCH, SEQ, D_MODEL), 1.0),
        'x_sample': nrm((DEC_BATCH, DEC_SEQ, D_MODEL), 1.0),
        'state_rwkv': nrm((DEC_BATCH, DEPTH, 2, RWKV_HEADS, RWKV_HEAD, RWKV_HEAD), 0.3),
        'c': nrm((DEC_BATCH, D_MODEL), 1.0),
        'c_ctx': nrm((D_MODEL,), 1.0),
        'w_ada': nrm((DEPTH, D_MODEL, 6 * D_MODEL), 0.02),
        'b_ada': nrm((DEPTH, 6 * D_MODEL), 0.02),
        'norm_mix': gain((DEPTH, D_MODEL)),
        'norm_ffn': gain((DEPTH, D_MODEL)),
        'w_in': nrm((DEPTH, D_MODEL, D_IN), D_MODEL ** -0.5),
        'conv_w': nrm((DEPTH, 3, D_IN), 0.2) + jnp.array([0.0, 1.0, 0.0], jnp.float32)[None, :, None],
        'w_out': nrm((DEPTH, D_MIX, D_MODEL), D_MIX ** -0.5),
        'rwkv_w0': jax.random.uniform(next(ks), (DEPTH, 2, D_RWKV), jnp.float32, -6.0, 1.0),
        'rwkv_w1': nrm((DEPTH, 2, D_MODEL, DECAY_LORA), D_MODEL ** -0.5),
        'rwkv_w2': nrm((DEPTH, 2, DECAY_LORA, D_RWKV), 0.1 * DECAY_LORA ** -0.5),
        'rwkv_a0': nrm((DEPTH, 2, D_RWKV), 0.1),
        'rwkv_a1': nrm((DEPTH, 2, D_MODEL, ICLR_LORA), D_MODEL ** -0.5),
        'rwkv_a2': nrm((DEPTH, 2, ICLR_LORA, D_RWKV), 0.3 * ICLR_LORA ** -0.5),
        'rwkv_g1': nrm((DEPTH, D_MODEL, GATE_LORA), D_MODEL ** -0.5),
        'rwkv_g2': nrm((DEPTH, GATE_LORA, D_RWKV), GATE_LORA ** -0.5),
        'rwkv_k_k': 0.85 + nrm((DEPTH, D_RWKV), 0.05),
        'rwkv_k_a': gain((DEPTH, D_RWKV)),
        'rwkv_r_k': nrm((DEPTH, 2, RWKV_HEADS, RWKV_HEAD), 0.1),
        'rwkv_ln_w': gain((DEPTH, D_RWKV)),
        'rwkv_ln_b': nrm((DEPTH, D_RWKV), 0.02),
        'hy_f_w1': nrm((DEPTH, FILTER_EMB, FILTER_HIDDEN), FILTER_EMB ** -0.5),
        'hy_f_b1': nrm((DEPTH, FILTER_HIDDEN), 0.1),
        'hy_f_w2': nrm((DEPTH, FILTER_HIDDEN, FILTER_HIDDEN), FILTER_HIDDEN ** -0.5),
        'hy_f_b2': nrm((DEPTH, FILTER_HIDDEN), 0.1),
        'hy_freq': gain((DEPTH, 2, FILTER_HIDDEN)),
        'hy_f_w3': nrm((DEPTH, FILTER_HIDDEN, 2 * HYENA_ORDER * D_HYENA), 0.1 * FILTER_HIDDEN ** -0.5),
        'hy_bias': nrm((DEPTH, HYENA_ORDER, D_HYENA), 0.1),
        'hy_norm': gain((DEPTH, D_HYENA)),
        'peer_wq': nrm((DEPTH, D_MODEL, PEER_HEADS * PEER_DKEY), D_MODEL ** -0.5),
        'peer_keys': nrm((DEPTH, 2, PEER_HEADS, N_KEYS, PEER_HALF), PEER_HALF ** -0.5),
        'peer_u': nrm((DEPTH, N_EXPERTS, D_MODEL), D_MODEL ** -0.5),
        'peer_v': nrm((DEPTH, N_EXPERTS, D_MODEL), 0.5),
        'final_norm': gain((D_MODEL,)),
    }

def reference(x_prompt, x_sample, state_rwkv, c, c_ctx, w_ada, b_ada, norm_mix, norm_ffn, w_in, conv_w, w_out,
              rwkv_w0, rwkv_w1, rwkv_w2, rwkv_a0, rwkv_a1, rwkv_a2, rwkv_g1, rwkv_g2, rwkv_k_k, rwkv_k_a,
              rwkv_r_k, rwkv_ln_w, rwkv_ln_b, hy_f_w1, hy_f_b1, hy_f_w2, hy_f_b2, hy_freq, hy_f_w3, hy_bias,
              hy_norm, peer_wq, peer_keys, peer_u, peer_v, final_norm):
    p = dict(norm_mix=norm_mix, norm_ffn=norm_ffn, w_in=w_in, conv_w=conv_w, w_out=w_out,
             rwkv_w0=rwkv_w0, rwkv_w1=rwkv_w1, rwkv_w2=rwkv_w2, rwkv_a0=rwkv_a0, rwkv_a1=rwkv_a1,
             rwkv_a2=rwkv_a2, rwkv_g1=rwkv_g1, rwkv_g2=rwkv_g2, rwkv_k_k=rwkv_k_k, rwkv_k_a=rwkv_k_a,
             rwkv_r_k=rwkv_r_k, rwkv_ln_w=rwkv_ln_w, rwkv_ln_b=rwkv_ln_b, hy_f_w1=hy_f_w1, hy_f_b1=hy_f_b1,
             hy_f_w2=hy_f_w2, hy_f_b2=hy_f_b2, hy_freq=hy_freq, hy_f_w3=hy_f_w3, hy_bias=hy_bias,
             hy_norm=hy_norm, peer_wq=peer_wq, peer_keys=peer_keys, peer_u=peer_u, peer_v=peer_v)
    xp = x_prompt
    xs = x_sample
    s_zero = jnp.zeros((xp.shape[0], 2, RWKV_HEADS, RWKV_HEAD, RWKV_HEAD), jnp.float32)
    new_states = []
    for l in range(DEPTH):
        mod_ctx = (jax.nn.silu(c_ctx) @ w_ada[l] + b_ada[l])[None, None, :]
        mod_lat = (jax.nn.silu(c) @ w_ada[l] + b_ada[l])[:, None, :]
        xp, s_ctx = layer(xp, mod_ctx, s_zero, None, p, l)
        xs, _ = layer(xs, mod_lat, state_rwkv[:, l], GRID_W, p, l)
        new_states.append(s_ctx.astype(xp.dtype))
    y_prompt = rmsnorm(xp, final_norm)
    y_sample = rmsnorm(xs, final_norm)
    new_state_rwkv = jnp.stack(new_states, axis=1)
    return (y_prompt, y_sample, new_state_rwkv)


_drawn_inputs = setup_inputs


def setup_inputs(seed=0):
    import zlib

    import numpy as np

    out = dict(_drawn_inputs(seed))
    spreads = {}
    factors = {'state_rwkv': 8.0,
     'rwkv_w1': 6.921,
     'rwkv_w2': 6.443,
     'rwkv_ln_w': 5.147,
     'rwkv_ln_b': 25.81,
     'hy_freq': 3.21,
     'hy_norm': 2.989,
     'norm_ffn': 3.393}
    for name, (base, spread) in spreads.items():
        noise = np.random.default_rng([zlib.crc32(name.encode()), seed]).standard_normal(out[name].shape)
        drawn = base * np.exp(spread * noise) if base else spread * noise
        out[name] = __import__('jax').numpy.asarray(drawn.astype(out[name].dtype))
    for name, factor in factors.items():
        out[name] = (out[name] * factor).astype(out[name].dtype)
    return out
```

```python
import math
from contextlib import ExitStack

import numpy as np

import concourse.bass as bass
from concourse import mybir

F32 = mybir.dt.float32
U32 = mybir.dt.uint32
ALU = mybir.AluOpType
ACT = mybir.ActivationFunctionType
AX = mybir.AxisListType

P = 128
D = 1024
KD = D // P
LC, LL = 128, 512
T = LC + LL
NT = T // P
NLT = LL // P
HD, HEADS = 64, 8
DR = HD * HEADS
PAIRS = DR // P
CH = 64
GRID = 64
NIN = 6 * DR // P
CONVROW = 80
LEVELS = 6
EXPH, TOPK, NKEY = 8, 16, 128
SLOTS = EXPH * TOPK
EPS, GN_EPS = 1e-6, 64e-5
SQD = math.exp(-0.5)
WBUF = 3
SB = 53200
RWLOADS = 13
UNITS = [(0, 0), (0, 1)] + [u for i in range(NLT) for u in ((1 + i, 0), (NLT - i, 1))]


class Own:

    def __init__(self, eng, chain):
        self.eng, self.chain, self.count, self.last, self.offset, self.passed = eng, chain, {}, None, 0, None

    def do(self, ins, sem=None):
        sem = sem or self.chain
        ins.then_inc(sem, 1)
        self.count[id(sem)] = self.count.get(id(sem), 0) + 1
        self.last = (sem, self.count[id(sem)])

    def settle(self):
        if isinstance(self.offset, int):
            self.eng.wait_ge(self.last[0], self.last[1] + self.offset)
        else:
            self.eng.wait_ge(self.last[0], self.last[1] + self.offset)
            self.eng.sem_inc(self.passed, 1)


RING = 16
ROUND = 1.5 * 2.0 ** 23
TWO_PI = (6.28125, 2 * math.pi - 6.28125)
PI_IN = 3.1415925


def SEQS(fctx, ictx, ftab, itab):
    yield [0], fctx[:, :, :].unsqueeze(2), ictx[:, :, :].unsqueeze(2)
    yield [1, 2, 3, 4], ftab, itab


def weight_chunks():
    order = [("ada", j) for j in range(4)]
    for j in range(6):
        order += [("in", j)] + [("ada", 4 + 2 * j + i) for i in range(2) if j < 4]
    return order + [("out", j) for j in range(2)] + [("wq", j) for j in range(4)]


def program(nc, a, outs):
    y_prompt, y_sample, new_state = outs
    WCH = weight_chunks()
    slot_of = {w: n % WBUF for n, w in enumerate(WCH)}
    turn_of = {w: n // WBUF for n, w in enumerate(WCH)}

    with ExitStack() as ctx:
        def sem(name):
            return ctx.enter_context(nc.semaphore(name))

        arena = ctx.enter_context(nc.sbuf_tensor("arena", [P, SB], F32))
        ps = ctx.enter_context(nc.psum_tensor("ps", [P, 8, 512], F32))

        def at(off, *shape):
            n = int(np.prod(shape))
            v = arena[:, off:off + n]
            if len(shape) == 2:
                v = v.rearrange("p (a b) -> p a b", b=shape[1])
            elif len(shape) == 3:
                v = v.rearrange("p (a b c) -> p a b c", b=shape[1], c=shape[2])
            elif len(shape) == 4:
                v = v.rearrange("p (a b c d) -> p a b c d", b=shape[1], c=shape[2], d=shape[3])
            return v

        class Region:
            def __init__(self, start, end):
                self.at_, self.end = start, end

            def __call__(self, *shape):
                v = at(self.at_, *shape)
                self.at_ += int(np.prod(shape))
                assert self.at_ <= self.end, (self.at_, self.end)
                return v

        keep = Region(0, 23000)
        ident = keep(P)
        x = keep(NT, D)
        hT = keep(KD, T)
        cols = keep(P)
        colsB = keep(P)
        csil = keep(2, KD)
        mod = keep(48, 2)
        amp = keep(KD, 2)
        stat = keep(64)
        hv = keep(NT, 3, DR)
        epsc = keep(4)
        w_end = keep.at_
        rw = Region(w_end, SB)
        rkv = rw(NT, 3, DR)
        KK = rw(NT, DR)
        Y = rw(NT, DR)
        yT = at(rw.at_ - 2 * NT * DR, 2, 4, T)
        bon = rw(NT, HEADS)
        tanhT, aloT, gateT = rw(T), rw(T), rw(T)
        vec = {n: rw(DR) for n in ("k_k", "k_a", "ln_w", "ln_b")}
        vec.update({n: rw(2, DR) for n in ("w0", "a0", "r_k")})
        lora1 = at(rw.at_ - 5 * 2 * DR, KD, 3 * P)
        sc = Region(rw.at_, SB)
        lm = at(ident.offset + P + NT * D, HEADS, 4, P)
        nn = sc(HEADS, 2, P)
        xs = sc(PAIRS, 2, 2, HD)
        tt = sc(PAIRS, 4, P)
        wsg, av, pi_, pinv, pex, kd, bt = (sc(DR) for _ in range(7))
        gblk = sc(2, PAIRS, P)
        hc = sc(2, PAIRS, P)
        qT = sc(PAIRS, P)
        st = sc(2, PAIRS, P)
        sn = sc(2, PAIRS, P)
        pc = sc(PAIRS, 2)
        hn = sc(4 * HEADS)
        tri = sc(2, 2, P)
        tot = sc(2)
        lmask = sc(2, 3, P)
        w2, a2 = (at(ident.offset + P + NT * D + 4096 + i * DR, DR) for i in range(2))
        i64 = sc(HD)
        g2 = at(rw.at_, DR)
        hy = Region(w_end, rw.at_)
        gf = hy(2, 2, 4, DR)
        yf = hy(2, 4, DR)
        win = hy(NT, DR)
        hid = hy(T)
        fw1, fw2 = hy(HD), hy(HD)
        fw3 = hy(4 * DR)
        htmp = hy(2, DR)
        fctx, ictx = hy(2, P), hy(2, P)
        zT = at(yf.offset, T)
        harg = at(yf.offset + T, 3, T)
        hnorm = at(win.offset, DR)
        gbc = at(gf.offset, 2, D)
        omul = at(gf.offset + 2 * D, 2, DR)
        pr = Region(w_end, rw.at_ + 2600)
        h2 = pr(NT, D)
        sco = pr(NT, 2 * EXPH, NKEY)
        qbuf = pr(2, T)
        keyT = pr(2 * EXPH, NKEY)
        eall = pr(NT, SLOTS).bitcast(U32)
        wall = pr(NT, SLOTS)
        g2bc = pr(2, D)
        assert pr.at_ <= SB - WBUF * KD * 512
        xn2 = at(sco.offset, NT, D)
        tk = Region(hv.offset, hv.offset + NT * 3 * DR)
        scur = tk(2 * EXPH, NKEY)
        cand = tk(EXPH, TOPK * TOPK)
        sv = tk(2 * EXPH, TOPK)
        si = tk(2 * EXPH, TOPK).bitcast(U32)
        sif = tk(2 * EXPH, TOPK)
        ts, tp, ti, tj, tf = (tk(EXPH, TOPK) for _ in range(5))
        tp, ti = tp.bitcast(U32), ti.bitcast(U32)
        eid = [tk(EXPH, TOPK) for _ in range(3)]
        iota16 = tk(TOPK)
        dots = tk(SLOTS)
        coef = tk(SLOTS)
        ibuf = [tk(SLOTS).bitcast(U32) for _ in range(2)]
        tsum = tk(2 * EXPH)
        onehot = at(scur.offset, EXPH, TOPK, TOPK)
        hbias = at(rw.at_ + DR, 2 * DR)[0:1, :]
        keyN = at(hv.offset, 2 * EXPH, NKEY)
        ring_at = SB - WBUF * KD * 512
        ring = [at(ring_at + i * KD * 512, KD, 512) for i in range(WBUF)]
        assert rw.at_ <= ring_at
        ftab = at(ring_at + KD * 512, 2, 4, DR)
        itab = at(ring_at + 2 * KD * 512, 2, 4, DR)
        hT_at = ident.offset + P + NT * D
        gslot = ([at(ring_at + i * D, D) for i in range(12)] + [at(hT_at + 4 * D, D)]
                 + [at(qbuf.offset + i * D, D) for i in range(3)])
        hcur = at(hT_at, D)
        acc = at(hT_at + D, 2, D)
        junk = at(hT_at + 3 * D, D).bitcast(mybir.dt.bfloat16).rearrange("p (a b) -> p a b", b=D)
        fnorm = at(sco.offset, D)
        sqj = at(sco.offset + D, NT, D)
        xn = at(w_end, NT, D)

        s = {}

        def S(name):
            if name not in s:
                s[name] = sem(name)
            return s[name]

        for n in ("ld_x", "ld_small", "ld_lora", "ld_vec", "pe_ch", "dve_ch", "act_ch", "pool_ch",
                  "rows_T", "cols_ok", "sig_c", "csil_ok", "ada_mm", "mod_ok", "sq_ok", "ms_ok", "rt_ok", "xn_ok",
                  "amp_ok", "xT_mm", "hT_ok", "in_mm", "conv_mid", "conv_ok", "uT_mm", "u_ok",                   "lora_mm", "lora_ok", "out_done"):
            S(n)
        row_here = [sem(f"row_here{i}") for i in range(RING)]
        wl = [sem(f"w_loaded{i}") for i in range(WBUF)]

        def w_free(eng, w):
            kind, j = w
            eng.wait_ge(*{"ada": (S("ada_mm"), j + 1), "in": (S("in_mm"), 4 * j + 4),
                          "out": (S("out_mm"), NT * (j + 1)), "wq": (S("q_mm"), 4 * j + 4)}[kind])

        def w_wait(eng, w):
            eng.wait_ge(wl[slot_of[w]], 16 * (turn_of[w] + 1))

        block = ctx.enter_context(nc.Block())

        @block.sync
        def _(sp):
            sp.dma_start(x[:, 0, :], a["x_prompt"][0]).then_inc(S("ld_x"), 16)
            sp.dma_start(cols, a["rows"][0:128, :]).then_inc(S("ld_small"), 16)
            sp.dma_start(colsB, a["rows"][128:256, :]).then_inc(S("ld_small"), 16)
            sp.dma_start(ident, a["ident"]).then_inc(S("ld_small"), 16)
            sp.dma_start(x[:, 1:NT, :], a["x_sample"][0].rearrange("(t p) d -> p t d", p=P)).then_inc(S("ld_x"), 16)
            src = {"ada": a["w_ada"], "in": a["w_in"], "out": a["w_out"], "wq": a["peer_wq"]}
            for n, (kind, j) in enumerate(WCH):
                if kind == "out":
                    break
                if n == 2:
                    for d in range(2):
                        sp.dma_start(lora1[:, :, 64 * d:64 * d + 64], a["rwkv_w1"][0, d].rearrange("(k p) n -> p k n", p=P)).then_inc(S("ld_lora"), 16)
                        sp.dma_start(lora1[:, :, 128 + 64 * d:192 + 64 * d], a["rwkv_a1"][0, d].rearrange("(k p) n -> p k n", p=P)).then_inc(S("ld_lora"), 16)
                    sp.dma_start(lora1[:, :, 256:384], a["rwkv_g1"][0].rearrange("(k p) n -> p k n", p=P)).then_inc(S("ld_lora"), 16)
                if n >= WBUF and n < 18:
                    w_free(sp, WCH[n - WBUF])
                w = src[kind][0, :, 512 * j:512 * j + 512].rearrange("(k p) n -> p k n", p=P)
                sp.dma_start(ring[n % WBUF], w).then_inc(wl[n % WBUF], 16)
            sp.wait_ge(S("lora_mm"), 3)
            ld = S("ld_rw")
            for nm in ("k_k", "k_a", "ln_w", "ln_b"):
                sp.dma_start(vec[nm], a["rwkv_" + nm][0].partition_broadcast(P)).then_inc(ld, 16)
            for nm in ("w0", "a0"):
                sp.dma_start(vec[nm], a["rwkv_" + nm][0].partition_broadcast(P)).then_inc(ld, 16)
            sp.dma_start(vec["r_k"], a["rwkv_r_k"][0].rearrange("d h j -> d (h j)").partition_broadcast(P)).then_inc(ld, 16)
            for dst, nm in ((w2, "rwkv_w2"), (a2, "rwkv_a2")):
                sp.dma_start(dst, a[nm][0].rearrange("d k n -> (d k) n")).then_inc(ld, 16)
            sp.dma_start(tri, a["tri"]).then_inc(ld, 16)
            sp.dma_start(tot, a["tot"]).then_inc(ld, 16)
            sp.dma_start(lmask, a["lmask"]).then_inc(ld, 16)
            sp.dma_start(i64, a["i64"]).then_inc(ld, 16)
            sp.wait_ge(S("sn_ok"), 1)
            for d in range(2):
                for h in range(HEADS):
                    i, p = h % 2, h // 2
                    sp.dma_start(new_state[0, 0, d, h], sn[64 * i:64 * i + 64, d, p, 64 * i:64 * i + 64]).then_inc(S("out_state"), 16)
            sp.wait_ge(S("out_state"), 16 * 16)
            for d in range(2):
                for h in range(HEADS):
                    i, p = h % 2, h // 2
                    sp.dma_start(sn[64 * i:64 * i + 64, d, p, 64 * i:64 * i + 64], a["state_rwkv"][0, 0, d, h]).then_inc(S("sn_in"), 16)
            sp.wait_ge(S("unit_ok"), len(UNITS))
            sp.dma_start(g2, a["rwkv_g2"][0]).then_inc(S("ld_g2"), 16)
            sp.dma_start(itab, a["itab"]).then_inc(S("ld_tab"), 16)
            sp.dma_start(ftab, a["ftab"]).then_inc(S("ld_tab"), 16)

            def load_w(n):
                kind, j = WCH[n]
                sp.dma_start(ring[n % WBUF], src[kind][0, :, 512 * j:512 * j + 512].rearrange("(k p) n -> p k n", p=P)).then_inc(wl[n % WBUF], 16)

            load_w(18)
            sp.wait_ge(S("ya_T"), 4)
            for dst, srcv in ((win, a["window"]), (zT[0:17, :], a["zT"]), (fw1[0:17, :], a["hy_f_w1"][0]), (fw2[0:64, :], a["hy_f_w2"][0]),
                              (fw3[0:64, :], a["hy_f_w3"][0]), (fctx, a["fctx"]), (ictx, a["ictx"])):
                sp.dma_start(dst, srcv).then_inc(S("ld_hy"), 16)
            sp.dma_start(hbias[:, :], a["hy_bias"][0].rearrange("o n -> (o n)").unsqueeze(0)).then_inc(S("ld_hy"), 16)
            sp.wait_ge(S("hf_ok"), 2 * NT)
            sp.dma_start(hnorm, a["hy_norm"][0].partition_broadcast(P)).then_inc(S("ld_hn"), 16)
            sp.wait_ge(S("hu_mm"), 2 * 5)
            load_w(19)
            sp.wait_ge(S("hi_mm"), 2 * 5)
            load_w(20)
            sp.wait_ge(S("out_mm"), NT)
            load_w(21)
            sp.wait_ge(S("out_mm"), 2 * NT)
            load_w(22)
            sp.dma_start(iota16, a["iota16"]).then_inc(S("ld_io"), 16)
            sp.dma_start(keyN, a["peer_keys"][0].rearrange("e h k d -> k (e h) d")).then_inc(S("ld_key"), 16)
            w_free(sp, WCH[20])
            load_w(23)
            sp.wait_ge(S("x3_ok"), NT)
            sp.dma_start(fnorm, a["final_norm"].partition_broadcast(P)).then_inc(S("ld_fn"), 16)
            sp.wait_ge(S("y_ok"), NT)
            sp.dma_start(y_prompt[0], x[:, 0, :]).then_inc(S("out_y"), 16)
            sp.dma_start(y_sample[0].rearrange("(t p) d -> p t d", p=P), x[:, 1:NT, :]).then_inc(S("out_y"), 16)
            sp.wait_ge(S("out_y"), 32)

        @block.tensor
        def _(pe):
            pe.wait_ge(S("ld_small"), 48)
            pe.transpose(ps[:, 0, 0:P], cols, ident)
            pe.transpose(ps[:, 0, P:2 * P], colsB, ident).then_inc(S("rows_T"), 1)

            def ada(j):
                w_wait(pe, ("ada", j))
                if j >= 2:
                    pe.wait_ge(S("mod_ok"), j - 1)
                for f in range(4):
                    o = ps[:, 6 + j % 2, 2 * f:2 * f + 2]
                    for k in range(KD):
                        m = pe.matmul(o, ring[slot_of["ada", j]][:, k, P * f:P * f + P], csil[:, :, k],
                                      start=(k == 0), stop=(k == KD - 1))
                m.then_inc(S("ada_mm"), 1)

            pe.wait_ge(S("csil_ok"), 1)
            for j in range(4):
                ada(j)

            def norm_T(first):
                pe.wait_ge(S("xn_ok"), first + 1)
                for k in range(KD):
                    n = first * KD + k
                    if n >= 3:
                        pe.wait_ge(S("hT_ok"), n - 2)
                    for t in range(NLT):
                        pe.transpose(ps[:, k % 3, P * t:P * t + P], xn[:, 1 + t, P * k:P * k + P], ident)
                    pe.transpose(ps[:, 3 + k % 3, 0:P], xn[:, 0, P * k:P * k + P], ident).then_inc(S("xT_mm"), 1)

            norm_T(0)
            pe.wait_ge(S("hT_ok"), KD)

            def to_rows(c):
                pe.wait_ge(S("conv_ok"), 4 * c + 4)
                for t in range(NT):
                    i = NT * c + t
                    if i >= 2:
                        pe.wait_ge(S("u_ok"), i - 1)
                    for f in range(4):
                        m = pe.transpose(ps[:, 4 + i % 2, P * f:P * f + P], yT[:, c % 2, f, P * t:P * t + P], ident)
                    m.then_inc(S("uT_mm"), 1)

            for n in range(NIN):
                c, f = divmod(n, 4)
                if f == 0:
                    w_wait(pe, ("in", c))
                if n >= 2:
                    pe.wait_ge(S("conv_ok"), n - 1)
                w = ring[slot_of["in", c]]
                for k in range(KD):
                    pe.matmul(ps[:, n % 2, :], w[:, k, P * f:P * f + P], hT[:, k, LC:T], start=(k == 0), stop=(k == KD - 1))
                for k in range(KD):
                    m = pe.matmul(ps[:, 2 + n % 2, 0:LC], w[:, k, P * f:P * f + P], hT[:, k, 0:LC], start=(k == 0), stop=(k == KD - 1))
                m.then_inc(S("in_mm"), 1)
                if f == 3 and c < 4:
                    ada(4 + 2 * c)
                    ada(5 + 2 * c)
                if f == 1 and c >= 1:
                    to_rows(c - 1)
            to_rows(5)
            pe.wait_ge(S("ld_lora"), 80)
            for i, (bl, bc) in enumerate(((0, 2), (1, 3), (4, 5))):
                if i == 0:
                    pe.wait_ge(S("conv_ok"), NIN)
                if i == 2:
                    pe.wait_ge(S("u_ok"), 6 * NT)
                for k in range(KD):
                    pe.matmul(ps[:, bl, :], lora1[:, k, P * i:P * i + P], hT[:, k, LC:T], start=(k == 0), stop=(k == KD - 1))
                for k in range(KD):
                    m = pe.matmul(ps[:, bc, 0:LC], lora1[:, k, P * i:P * i + P], hT[:, k, 0:LC], start=(k == 0), stop=(k == KD - 1))
                m.then_inc(S("lora_mm"), 1)
            pe.wait_ge(S("ld_rw"), 16 * RWLOADS)
            pe.wait_ge(S("lora_ok"), 3)
            for n, (t, d) in enumerate(UNITS):
                if n >= 1:
                    pe.wait_ge(S("unit_ok"), n)
                    pe.wait_ge(S("r_hc"), n)
                if n == 2:
                    pe.wait_ge(S("sn_in"), 16 * 16)
                    for e in range(2):
                        for p in range(PAIRS):
                            m = pe.transpose(ps[:, 0 + e, P * p:P * p + P], sn[:, e, p, :], ident)
                    m.then_inc(S("st_mm"), 1)
                    pe.wait_ge(S("st_in"), 1)
                pe.matmul(ps[:, 0, :], tanhT[64 * d:64 * d + 64, P * t:P * t + P], w2[64 * d:64 * d + 64, :], start=True, stop=True)
                pe.matmul(ps[:, 1, :], aloT[64 * d:64 * d + 64, P * t:P * t + P], a2[64 * d:64 * d + 64, :], start=True, stop=True).then_inc(S("r_lora"), 1)
                pe.wait_ge(S("r_sig"), 2 * n + 1)
                pe.matmul(ps[:, 2, :], tri[:, d, 0, :], wsg, start=True, stop=True)
                pe.matmul(ps[:, 3, :], tri[:, d, 1, :], wsg, start=True, stop=True)
                for p in range(PAIRS):
                    m = pe.matmul(ps[:, 4, 2 * p:2 * p + 2], wsg[:, P * p:P * p + P], tot, start=True, stop=True)
                m.then_inc(S("r_cum"), 1)
                pe.wait_ge(S("r_ops"), n + 1)
                for p in range(PAIRS):
                    if p == 0:
                        pe.wait_ge(S("r_exp"), 4 * n + 4)
                    for i, v in enumerate((pex, pi_, bt, kd)):
                        m = pe.transpose(ps[:, 4 + p, P * i:P * i + P], v[:, P * p:P * p + P], ident)
                    m.then_inc(S("r_tr"), 1)
                for p in range(PAIRS):
                    pe.wait_ge(S("r_tt"), 4 * n + (p + 1 if p != 1 else 4))
                    if p >= 2:
                        pe.wait_ge(S("r_mask"), 4 * n + p - 1)
                    b = 4 * (p % 2)
                    for i in range(2):
                        q = slice(64 * i, 64 * i + 64)
                        ar = tt[q, p, 0:2, :]
                        pe.matmul(ps[:, b + i, 0:256], tt[q, p, 2, :], ar, start=True, stop=True)
                        pe.matmul(ps[:, b + i, 256:512], tt[q, p, 3, :], ar, start=True, stop=True)
                        m = pe.matmul(ps[:, b + 2 + i, 0:P], tt[q, p, 0, :], tt[q, p, 2, :], start=True, stop=True)
                    m.then_inc(S("r_s1"), 1)
                pe.wait_ge(S("r_mask"), 4 * n + 4)
                for h in range(HEADS):
                    m = pe.matmul(ps[:, 0, 64 * h:64 * h + 64], lm[:, h, 2, :], rkv[:, t, 2, 64 * h:64 * h + 64], start=True, stop=True)
                m.then_inc(S("r_s2"), 1)
                for l in range(LEVELS):
                    for g in range(2):
                        if l == 0:
                            pe.wait_ge(S("r_x0"), 2 * n + 2)
                        else:
                            pe.wait_ge(S("r_lvx"), 12 * n + 2 * (l - 1) + g + 1)
                            pe.wait_ge(S("r_lvn"), 10 * n + 2 * (l - 1) + g + 1)
                        for j in range(4):
                            h = 4 * g + j
                            nT = lm[:, h, 0, :] if l == 0 else nn[:, h, 1, :]
                            q = slice(P * j, P * j + P)
                            m = pe.matmul(ps[:, 1 + 3 * g, :].rearrange("p (u k i j) -> p u k i j", u=2, k=2, i=2)[:, j // 2, :, j % 2, :], nT,
                                          xs[:, h // 2, :, h % 2, :], start=True, stop=True)
                            if l < LEVELS - 1:
                                pe.matmul(ps[:, 2 + 3 * g, q], nT, nn[:, h, 0, :], start=True, stop=True)
                                m = pe.matmul(ps[:, 3 + 3 * g, q], nn[:, h, 0, :], nT, start=True, stop=True)
                        m.then_inc(S("r_lv"), 1)
                pe.wait_ge(S("r_lvx"), 12 * n + 12)
                pe.wait_ge(S("r_lvn"), 10 * n + 10)
                for p in range(PAIRS):
                    f = slice(P * p, P * p + P)
                    for c in range(2):
                        q = slice(64 * c, 64 * c + 64)
                        m = pe.matmul(ps[:, 7 * c, f], xs[q, p, 0, :, :].rearrange("p a b -> p (a b)"), bt[q, f], start=True, stop=True)
                m.then_inc(S("r_g"), 1)
                for h in range(HEADS):
                    i, p = h % 2, h // 2
                    m = pe.matmul(ps[64 * i:64 * i + 64, 1, P * p:P * p + P], xs[:, p, 0, i, :], lm[:, h, 1, :], start=True, stop=True)
                m.then_inc(S("r_q"), 1)
                for p in range(PAIRS):
                    f = slice(P * p, P * p + P)
                    for c in range(2):
                        q = slice(64 * c, 64 * c + 64)
                        pe.matmul(ps[:, 2 + c, f], kd[q, f], rkv[q, t, 2, f], start=True, stop=False)
                        m = pe.matmul(ps[:, 2 + c, f], bt[q, f], xs[q, p, 1, :, :].rearrange("p a b -> p (a b)"), start=False, stop=True)
                m.then_inc(S("r_hm"), 1)
                for h in range(HEADS):
                    f = slice(64 * h, 64 * h + 64)
                    pe.matmul(ps[:, 5, f], lm[:, h, 3, :], rkv[:, t, 2, f], start=True, stop=False)
                    m = pe.matmul(ps[:, 5, f], lm[:, h, 1, :], xs[:, h // 2, 1, h % 2, :], start=False, stop=True)
                m.then_inc(S("r_yl"), 1)
                pe.wait_ge(S("r_gq"), n + 1)
                for k, c in enumerate((0, 1) if d == 0 else (1, 0)):
                    if n >= 1 or k:
                        pe.wait_ge(S("r_st"), 2 * n + k)
                    for p in range(PAIRS):
                        f = slice(P * p, P * p + P)
                        m = pe.matmul(ps[:, 4, f], gblk[:, c, p, :], st[:, d, p, :], start=True, stop=True)
                    for p in range(PAIRS):
                        m = pe.matmul(ps[64 * c:64 * c + 64, 6, P * p:P * p + P], qT[:, p, 64 * c:64 * c + 64], st[:, d, p, :], start=True, stop=True)
                    m.then_inc(S("r_step"), 1)
                if n == 1:
                    pe.wait_ge(S("r_st"), 4)
                    pe.wait_ge(S("unit_ok"), 2)
                    for e in range(2):
                        for p in range(PAIRS):
                            m = pe.transpose(ps[:, 2 + e, P * p:P * p + P], st[:, e, p, :], ident)
                    m.then_inc(S("sn_mm"), 1)
                    pe.wait_ge(S("sn_ok"), 1)
            pe.wait_ge(S("unit_ok"), len(UNITS))
            pe.wait_ge(S("ld_g2"), 16)
            for t in range(NT):
                if t >= 2:
                    pe.wait_ge(S("gm_ok"), t - 1)
                pe.matmul(ps[:, t % 2, :], gateT[:, P * t:P * t + P], g2, start=True, stop=True).then_inc(S("g_mm"), 1)

            def mix_T(which, ok):
                for k in range(4):
                    if k == 0:
                        pe.wait_ge(ok, NT)
                    if k >= 2:
                        pe.wait_ge(S("mix_ok"), 4 * which + k - 1)
                    elif which:
                        pe.wait_ge(S("mix_ok"), 4)
                    for t in range(NT):
                        v = hv[:, t, 0, P * k:P * k + P] if which else Y[:, t, P * k:P * k + P]
                        b = (2 + 2 * (k % 2), P * (t - 1)) if t else (3 + 2 * (k % 2), 0)
                        m = pe.transpose(ps[:, b[0], b[1]:b[1] + P], v, ident)
                    m.then_inc(S("yb_T" if which else "ya_T"), 1)

            mix_T(0, S("gm_ok"))
            pe.wait_ge(S("ld_hy"), 8 * 16)
            pe.wait_ge(S("gm_ok"), NT)
            pe.wait_ge(S("mix_ok"), 4)
            pe.matmul(ps[0:HD, 0, :], fw1[0:17, :], zT[0:17, 0:LL], start=True, stop=True)
            pe.matmul(ps[0:HD, 1, 0:LC], fw1[0:17, :], zT[0:17, LL:T], start=True, stop=True).then_inc(S("hid_mm"), 1)
            pe.wait_ge(S("sin_ok"), 1)
            pe.matmul(ps[0:HD, 0, :], fw2[0:HD, :], hid[0:HD, 0:LL], start=True, stop=True)
            pe.matmul(ps[0:HD, 1, 0:LC], fw2[0:HD, :], hid[0:HD, LL:T], start=True, stop=True).then_inc(S("hid_mm"), 1)
            pe.wait_ge(S("sin_ok"), 2)
            pe.wait_ge(S("ld_tab"), 32)
            nf = ng = nu = ni = 0
            for tiles, fcs, ics in SEQS(fctx, ictx, ftab, itab):
                nk = len(tiles)
                for o in range(2):
                    for t in tiles:
                        b = 2 * (nf % 2)
                        if nf >= 2:
                            pe.wait_ge(S("hf_ok"), nf - 1)
                        pos = slice(LL, T) if t == 0 else slice(P * (t - 1), P * t)
                        for e in range(2):
                            q = slice(DR * (2 * o + e), DR * (2 * o + e) + DR)
                            m = pe.matmul(ps[:, b + e, :], hid[0:HD, pos], fw3[0:HD, q], start=True, stop=True)
                        m.then_inc(S("hf_mm"), 1)
                        nf += 1
                    pe.wait_ge(S("hf_ok"), nf)
                    for k in range(nk):
                        b = 4 + 2 * (ng % 2)
                        if ng >= 2:
                            pe.wait_ge(S("hg_ok"), ng - 1)
                        for e in range(2):
                            for j in range(nk):
                                m = pe.matmul(ps[:, b + e, :], fcs[:, e, j, P * k:P * k + P], yf[:, e, j, :], start=(j == 0), stop=(j == nk - 1))
                        m.then_inc(S("hg_mm"), 1)
                        ng += 1
                for o in range(2):
                    if o:
                        pe.wait_ge(S("hz_ok"), ni)
                    pe.wait_ge(S("hg_ok"), ng)
                    for k in range(nk):
                        b = 2 * (nu % 2)
                        if nu >= 2:
                            pe.wait_ge(S("hy_ok"), nu - 1)
                        for e in range(2):
                            for j, t in enumerate(tiles):
                                m = pe.matmul(ps[:, b + e, :], fcs[:, e, j, P * k:P * k + P], hv[:, t, 0, :], start=(j == 0), stop=(j == nk - 1))
                        m.then_inc(S("hu_mm"), 1)
                        nu += 1
                    pe.wait_ge(S("hy_ok"), nu)
                    for j in range(nk):
                        if ni >= 2:
                            pe.wait_ge(S("hz_ok"), ni - 1)
                        for e in range(2):
                            for k in range(nk):
                                m = pe.matmul(ps[:, 4 + ni % 2, :], ics[:, e, k, P * j:P * j + P], yf[:, e, k, :],
                                              start=(e == 0 and k == 0), stop=(e == 1 and k == nk - 1))
                        m.then_inc(S("hi_mm"), 1)
                        ni += 1
            pe.wait_ge(S("hz_ok"), ni)

            def spread(first, src_col, bank):
                for c in range(2):
                    for k in range(KD):
                        m = pe.matmul(ps[:, bank + 2 * c + k // 4, P * (k % 4):P * (k % 4) + P],
                                      mod[:, src_col + k, c:c + 1].to_broadcast([P, P]), ident, start=True, stop=True)
                m.then_inc(S("gate_mm"), 1)

            mix_T(1, S("yb_ok"))
            pe.wait_ge(S("mix_ok"), 8)
            pe.wait_ge(S("mod_ok"), 12)
            spread(0, 16, 0)
            pe.wait_ge(S("gate_ok"), 1)
            for j in range(2):
                w_wait(pe, ("out", j))
                for t in range(NT):
                    i = NT * j + t
                    if i >= 2:
                        pe.wait_ge(S("x2_ok"), i - 1)
                    for k in range(KD):
                        m = pe.matmul(ps[:, 4 + i % 2, :], hT[:, k, P * t:P * t + P], ring[slot_of["out", j]][:, k, :], start=(k == 0), stop=(k == KD - 1))
                    m.then_inc(S("out_mm"), 1)
            pe.wait_ge(S("x2_ok"), 2 * NT)
            norm_T(1)
            pe.wait_ge(S("hT_ok"), 2 * KD)
            spread(1, 40, 0)
            pe.wait_ge(S("gate_ok"), 2)
            for t in range(NT):
                for k in range(KD):
                    if k % 4 == 0:
                        i = 2 * t + k // 4
                        if i >= 2:
                            pe.wait_ge(S("h2_ok"), i - 1)
                    m = pe.transpose(ps[:, i % 2, P * (k % 4):P * (k % 4) + P], hT[:, k, P * t:P * t + P], ident)
                    if k % 4 == 3:
                        m.then_inc(S("h2_mm"), 1)
            pe.wait_ge(S("ld_key"), 16)
            for g in range(4):
                for i in range(4):
                    hh = 4 * g + i
                    m = pe.transpose(ps[:, 2 + g, P * i:P * i + P], keyN[:, EXPH * (hh % 2) + hh // 2, :], ident)
                m.then_inc(S("key_mm"), 1)
            pe.wait_ge(S("h2_ok"), 2 * NT)
            pe.wait_ge(S("key_ok"), 4)

            def scores(n):
                pe.wait_ge(S("q_ok"), n + 1)
                if n >= 1:
                    pe.wait_ge(S("sc_ok"), n)
                for t in range(NT):
                    b = (6, P * (t - 1)) if t else (7, 0)
                    m = pe.matmul(ps[:, b[0], b[1]:b[1] + P], qbuf[:, n % 2, P * t:P * t + P], keyT[:, n, :], start=True, stop=True)
                m.then_inc(S("sc_mm"), 1)

            for n in range(2 * EXPH):
                j, f = divmod(n, 4)
                if f == 0:
                    w_wait(pe, ("wq", j))
                if n >= 2:
                    pe.wait_ge(S("q_ok"), n - 1)
                w = ring[slot_of["wq", j]]
                for k in range(KD):
                    pe.matmul(ps[:, n % 2, :], w[:, k, P * f:P * f + P], hT[:, k, LC:T], start=(k == 0), stop=(k == KD - 1))
                for k in range(KD):
                    m = pe.matmul(ps[:, 2 + n % 2, 0:LC], w[:, k, P * f:P * f + P], hT[:, k, 0:LC], start=(k == 0), stop=(k == KD - 1))
                m.then_inc(S("q_mm"), 1)
                if n >= 1:
                    scores(n - 1)
            scores(2 * EXPH - 1)

        @block.scalar
        def _(act):
            own = Own(act, S("act_ch"))
            A = act.activation
            act.wait_ge(S("cols_ok"), 1)
            own.do(A(csil[:, :, :].rearrange("p a b -> p (a b)"), cols[:, 48:64], ACT.Sigmoid), S("sig_c"))

            def norm_sq(first):
                for t in range(NT):
                    own.do(A(xn[:, t, :], x[:, t, :], ACT.Square, accum_out=stat[:, t:t + 1]), S("sq_ok"))
                act.wait_ge(S("ms_ok"), first + 1)
                own.do(A(stat[:, 16:16 + NT], stat[:, 8:8 + NT], ACT.Sqrt), S("rt_ok"))

            act.wait_ge(S("ld_x"), 32)
            norm_sq(0)

            def norm_mod(first, shift):
                act.wait_ge(S("amp_ok"), first + 1)
                for k in range(KD):
                    act.wait_ge(S("xT_mm"), first * KD + k + 1)
                    A(hT[:, k, LC:T], ps[:, k % 3, :], ACT.Identity, bias=mod[:, shift + k, 1:2], scale=amp[:, k, 1:2])
                    own.do(A(hT[:, k, 0:LC], ps[:, 3 + k % 3, 0:P], ACT.Identity, bias=mod[:, shift + k, 0:1],
                             scale=amp[:, k, 0:1]), S("hT_ok"))

            norm_mod(0, 0)

            def rows_out(c):
                for t in range(NT):
                    i = NT * c + t
                    act.wait_ge(S("uT_mm"), i + 1)
                    dst = rkv[:, t, c, :] if c < 3 else hv[:, t, c - 3, :]
                    own.do(A(dst, ps[:, 4 + i % 2, :], ACT.Copy), S("u_ok"))

            for n in range(NIN):
                c, f = divmod(n, 4)
                act.wait_ge(S("in_mm"), n + 1)
                if c >= 2 and f == 0:
                    act.wait_ge(S("uT_mm"), NT * (c - 1))
                w1 = colsB[:, NIN + n:NIN + n + 1]
                A(yT[:, c % 2, f, LC:T], ps[:, n % 2, :], ACT.Copy, scale=w1)
                own.do(A(yT[:, c % 2, f, 0:LC], ps[:, 2 + n % 2, 0:LC], ACT.Copy, scale=w1), S("conv_mid"))
                if f == 1 and c >= 1:
                    rows_out(c - 1)
            rows_out(5)
            for i, (bl, bc, dst, fn) in enumerate(((0, 2, tanhT, ACT.Tanh), (1, 3, aloT, ACT.Copy), (4, 5, gateT, ACT.Sigmoid))):
                act.wait_ge(S("lora_mm"), i + 1)
                A(dst[:, LC:T], ps[:, bl, :], fn)
                own.do(A(dst[:, 0:LC], ps[:, bc, 0:LC], fn), S("lora_ok"))
            act.wait_ge(S("kk_sq"), 1)
            own.do(A(bon[:, :, :].rearrange("p a b -> p (a b)"), bon[:, :, :].rearrange("p a b -> p (a b)"), ACT.Sqrt), S("kk_rt"))
            for n, (t, d) in enumerate(UNITS):
                act.wait_ge(S("r_pre"), 2 * n + 1)
                own.do(A(wsg, wsg, ACT.Sigmoid), S("r_sig"))
                act.wait_ge(S("r_pre"), 2 * n + 2)
                own.do(A(av, av, ACT.Sigmoid), S("r_sig"))
                act.wait_ge(S("r_cum"), n + 1)
                own.do(A(pi_, ps[:, 2, :], ACT.Exp), S("r_exp"))
                own.do(A(pinv, ps[:, 2, :], ACT.Exp, scale=-1.0), S("r_exp"))
                own.do(A(pex, ps[:, 3, :], ACT.Exp), S("r_exp"))
                own.do(A(pc[:, :, :].rearrange("p a b -> p (a b)"), ps[:, 4, 0:2 * PAIRS], ACT.Exp), S("r_exp"))
                act.wait_ge(S("r_ops"), n + 1)
                if n >= 1:
                    act.wait_ge(S("r_yl"), n)
                own.do(A(xs[:, :, 0, :, :].rearrange("p u i j -> p u (i j)"), pex.rearrange("p (u x) -> p u x", x=P), ACT.Copy), S("r_x0"))
                for p in range(PAIRS):
                    act.wait_ge(S("r_tr"), 4 * n + p + 1)
                    own.do(A(tt[:, p, :, :].rearrange("p a b -> p (a b)"), ps[:, 4 + p, :], ACT.Copy), S("r_tt"))
                act.wait_ge(S("r_s2"), n + 1)
                own.do(A(xs[:, :, 1, :, :].rearrange("p u i j -> p u (i j)"), ps[:, 0, :].rearrange("p (u x) -> p u x", x=P), ACT.Copy), S("r_x0"))
                for l in range(LEVELS - 1):
                    for g in range(2):
                        act.wait_ge(S("r_lv"), 12 * n + 2 * l + g + 1)
                        own.do(A(nn[:, 4 * g:4 * g + 4, :, :].rearrange("p h i t -> p i h t"),
                                 ps[:, 2 + 3 * g:4 + 3 * g, :].rearrange("p i (h t) -> p i h t", t=P), ACT.Copy), S("r_lvn"))
                act.wait_ge(S("r_hm"), n + 1)
                if n >= 1:
                    act.wait_ge(S("r_st"), 2 * n)
                for i in range(2):
                    q = slice(64 * i, 64 * i + 64)
                    m = A(hc[q, :, :, 64 * i:64 * i + 64], ps[q, 2:4, :].rearrange("p c (a b) -> p c a b", b=P)[:, :, :, 64 * i:64 * i + 64], ACT.Copy)
                own.do(m, S("r_hc"))
            act.wait_ge(S("gn_var"), 1)
            own.do(A(KK[:, 0, 0:40], KK[:, 0, 0:40], ACT.Sqrt), S("gn_rt"))

            def mix_out(which):
                for k in range(4):
                    act.wait_ge(S("yb_T" if which else "ya_T"), k + 1)
                    A(hT[:, 4 * which + k, LC:T], ps[:, 2 + 2 * (k % 2), :], ACT.Copy)
                    own.do(A(hT[:, 4 * which + k, 0:LC], ps[:, 3 + 2 * (k % 2), 0:LC], ACT.Copy), S("mix_ok"))

            mix_out(0)
            for i in range(2):
                act.wait_ge(S("arg_ok"), i + 1)
                own.do(A(hid[0:HD, :], harg[0:HD, 2, :], ACT.Sin), S("sin_ok"))
            ng = 0
            for tiles, _, _ in SEQS(fctx, ictx, ftab, itab):
                for o in range(2):
                    for k in range(len(tiles)):
                        act.wait_ge(S("hg_mm"), ng + 1)
                        b = 4 + 2 * (ng % 2)
                        if len(tiles) > 1 and k == 0 and o == 0:
                            act.wait_ge(S("hy_ok"), 2)
                        own.do(A(gf[:, o, :, k, :], ps[:, b:b + 2, :], ACT.Copy), S("hg_ok"))
                        ng += 1
            act.wait_ge(S("hz_ok"), 2 * NT)
            act.wait_ge(S("hy_ok"), 2 * NT)
            for t in range(NT):
                own.do(A(yf[:, 0, t % 4, :] if t < 4 else yf[:, 1, 0, :], hv[:, t, 0, :], ACT.Square, accum_out=stat[:, 32 + t:33 + t]), S("zsq_ok"))
            act.wait_ge(S("zms_ok"), 1)
            own.do(A(stat[:, 48:48 + NT], stat[:, 40:40 + NT], ACT.Sqrt), S("zrt_ok"))
            mix_out(1)
            act.wait_ge(S("gate_mm"), 1)
            own.do(A(gbc[:, :, :].rearrange("p c n -> p (c n)"), ps[:, 0:4, :].rearrange("p a b -> p (a b)"), ACT.Copy), S("gate_ok"))
            act.wait_ge(S("x2_ok"), 2 * NT)
            norm_sq(1)
            norm_mod(1, 24)
            act.wait_ge(S("gate_mm"), 2)
            own.do(A(g2bc[:, :, :].rearrange("p c n -> p (c n)"), ps[:, 0:4, :].rearrange("p a b -> p (a b)"), ACT.Copy), S("gate_ok"))
            for i in range(2 * NT):
                act.wait_ge(S("h2_mm"), i + 1)
                own.do(A(h2[:, i // 2, 512 * (i % 2):512 * (i % 2) + 512], ps[:, i % 2, :], ACT.Copy), S("h2_ok"))
            for g in range(4):
                act.wait_ge(S("key_mm"), g + 1)
                own.do(A(keyT[:, 4 * g:4 * g + 4, :].rearrange("p a b -> p (a b)"), ps[:, 2 + g, :], ACT.Copy), S("key_ok"))

            def sc_out(n):
                act.wait_ge(S("sc_mm"), n + 1)
                A(sco[:, 1:NT, n, :], ps[:, 6, :].rearrange("p (t k) -> p t k", k=NKEY), ACT.Copy)
                own.do(A(sco[:, 0, n, :], ps[:, 7, 0:NKEY], ACT.Copy), S("sc_ok"))

            for n in range(2 * EXPH):
                act.wait_ge(S("q_mm"), n + 1)
                if n >= 2:
                    act.wait_ge(S("sc_mm"), n - 1)
                A(qbuf[:, n % 2, LC:T], ps[:, n % 2, :], ACT.Copy)
                own.do(A(qbuf[:, n % 2, 0:LC], ps[:, 2 + n % 2, 0:LC], ACT.Copy), S("q_ok"))
                if n >= 1:
                    sc_out(n - 1)
            sc_out(2 * EXPH - 1)
            tsf = ts[:, :, :].rearrange("p a b -> p (a b)")

            act.wait_ge(S("top_sub"), 1)
            A(tsf, tsf, ACT.Exp).then_inc(S("top_exp"), 1)
            with act.Fori(0, NT - 1) as i:
                act.wait_ge(S("g_used"), i * (2 * SLOTS) + RING + SLOTS)
                A(dots, dots, ACT.Gelu).then_inc(S("gelu_ok"), 1)
                act.wait_ge(S("top_sub"), i + 2)
                A(tsf, tsf, ACT.Exp).then_inc(S("top_exp"), 1)
            act.wait_ge(S("g_used"), (NT - 1) * 2 * SLOTS + RING + SLOTS)
            A(dots, dots, ACT.Gelu).then_inc(S("gelu_ok"), 1)
            act.wait_ge(S("x3_ok"), NT)
            for t in range(NT):
                A(sqj[:, t, :], x[:, t, :], ACT.Square, accum_out=stat[:, t:t + 1]).then_inc(S("fsq_ok"), 1)
            act.wait_ge(S("fms_ok"), 1)
            A(stat[:, 16:16 + NT], stat[:, 8:8 + NT], ACT.Sqrt).then_inc(S("frt_ok"), 1)

        @block.vector
        def _(dve):
            own = Own(dve, S("dve_ch"))
            V = dve
            dve.wait_ge(S("rows_T"), 1)
            V.tensor_copy(cols, ps[:, 0, 0:P])
            own.do(V.tensor_copy(colsB, ps[:, 0, P:2 * P]), S("cols_ok"))
            dve.wait_ge(S("sig_c"), 1)
            own.settle()
            cs = csil.rearrange("p a b -> p (a b)")
            own.do(V.tensor_tensor(cs, cs, cols[:, 48:64], ALU.mult), S("csil_ok"))

            def norm_rows(first):
                dve.wait_ge(S("sq_ok"), NT * (first + 1))
                own.do(V.tensor_scalar(stat[:, 8:8 + NT], stat[:, 0:NT], 1.0 / D, EPS, ALU.mult, ALU.add), S("ms_ok"))
                dve.wait_ge(S("rt_ok"), first + 1)
                own.do(V.reciprocal(stat[:, 24:24 + NT], stat[:, 16:16 + NT]))
                own.settle()
                for t in range(NT):
                    i = V.tensor_scalar(xn[:, t, :], x[:, t, :], stat[:, 24 + t:25 + t], None, ALU.mult)
                own.do(i, S("xn_ok"))

            norm_rows(0)

            def mod_out(j):
                dve.wait_ge(S("ada_mm"), j + 1)
                o = mod[:, 4 * j:4 * j + 4, :]
                own.do(V.tensor_tensor(o, ps[:, 6 + j % 2, 0:8].rearrange("p (a b) -> p a b", b=2),
                                       cols[:, 4 * j:4 * j + 4].unsqueeze(2).to_broadcast([P, 4, 2]), ALU.add), S("mod_ok"))

            def amplitude(scale, gain):
                own.settle()
                own.do(V.scalar_tensor_tensor(amp, mod[:, scale:scale + KD, :], 1.0,
                                              cols[:, gain:gain + KD].unsqueeze(2).to_broadcast([P, KD, 2]),
                                              ALU.add, ALU.mult), S("amp_ok"))

            for j in range(4):
                mod_out(j)
            amplitude(8, 64)
            for n in range(NIN):
                c, f = divmod(n, 4)
                dve.wait_ge(S("conv_mid"), n + 1)
                for j, (shift_o, shift_i) in enumerate(((1, 0), (0, 1))):
                    w = colsB[:, (0, 2)[j] * NIN + n:(0, 2)[j] * NIN + n + 1]
                    lat = yT[:, c % 2, f, LC:T].rearrange("p (r g) -> p r g", g=GRID)
                    lin = ps[:, n % 2, :].rearrange("p (r g) -> p r g", g=GRID)
                    o = lat[:, :, shift_o:shift_o + GRID - 1]
                    if j:
                        own.settle()
                    own.do(V.scalar_tensor_tensor(o, lin[:, :, shift_i:shift_i + GRID - 1], w, o, ALU.mult, ALU.add))
                    o = yT[:, c % 2, f, shift_o:shift_o + LC - 1]
                    own.do(V.scalar_tensor_tensor(o, ps[:, 2 + n % 2, shift_i:shift_i + LC - 1], w, o, ALU.mult, ALU.add),
                           S("conv_ok") if j else None)
                if f == 3 and c < 4:
                    mod_out(4 + 2 * c)
                    mod_out(5 + 2 * c)
            bonf = bon[:, :, :].rearrange("p a b -> p (a b)")
            dve.wait_ge(S("u_ok"), 6 * NT)
            dve.wait_ge(S("lora_ok"), 3)
            dve.wait_ge(S("ld_rw"), 16 * RWLOADS)
            for t in range(NT):
                own.do(V.tensor_tensor(KK[:, t, :], rkv[:, t, 1, :], vec["k_k"], ALU.mult))
            own.settle()
            sq = Y[:, :, :].rearrange("p t (h j) -> p t h j", j=HD)
            own.do(V.tensor_tensor(Y, KK, KK, ALU.mult))
            own.settle()
            own.do(V.tensor_reduce(bon, sq, AX.X, ALU.add))
            own.settle()
            own.do(V.tensor_scalar(bonf, bonf, 1e-24, None, ALU.max), S("kk_sq"))
            dve.wait_ge(S("kk_rt"), 1)
            own.do(V.reciprocal(bonf, bonf))
            own.settle()
            for t in range(NT):
                k = KK[:, t, :].rearrange("p (h j) -> p h j", j=HD)
                own.do(V.tensor_tensor(k, k, bon[:, t, :].unsqueeze(2).to_broadcast([P, HEADS, HD]), ALU.mult))
            own.settle()
            V.memset(bonf, 0.0)
            V.memset(Y, 0.0)
            V.memset(gblk, 0.0)
            V.memset(st, 0.0)
            own.do(V.memset(hc, 0.0), S("rw_zero"))
            own.settle()
            for n, (t, d) in enumerate(UNITS):
                R, K = rkv[:, t, 0, :], rkv[:, t, 1, :]
                if n == 2:
                    dve.wait_ge(S("st_mm"), 1)
                    own.do(V.tensor_copy(st[:, :, :, :].rearrange("p e a b -> p e (a b)"), ps[:, 0:2, :]), S("st_in"))
                dve.wait_ge(S("r_lora"), n + 1)
                own.do(V.tensor_tensor(wsg, ps[:, 0, :], vec["w0"][:, d, :], ALU.add), S("r_pre"))
                own.do(V.tensor_tensor(av, ps[:, 1, :], vec["a0"][:, d, :], ALU.add), S("r_pre"))
                dve.wait_ge(S("r_sig"), 2 * n + 2)
                own.do(V.scalar_tensor_tensor(kd, av, -1.0, vec["k_a"], ALU.add, ALU.mult))
                own.settle()
                own.do(V.scalar_tensor_tensor(kd, kd, 1.0, K, ALU.add, ALU.mult))
                own.settle()
                own.do(V.tensor_tensor(bt, kd, R, ALU.mult))
                own.settle()
                own.do(V.tensor_tensor(bt, bt, vec["r_k"][:, d, :], ALU.mult))
                own.settle()
                own.do(V.tensor_reduce(hn[:, 0:HEADS], bt.rearrange("p (h j) -> p h j", j=HD), AX.X, ALU.add))
                own.do(V.tensor_tensor(av, av, KK[:, t, :], ALU.mult))
                own.settle()
                own.do(V.tensor_tensor(bon[:, t, :], bon[:, t, :], hn[:, 0:HEADS], ALU.add))
                dve.wait_ge(S("r_exp"), 4 * n + 4)
                V.scalar_tensor_tensor(bt, av, -1.0, pinv, ALU.mult, ALU.mult)
                V.tensor_tensor(pex, pex, KK[:, t, :], ALU.mult)
                V.tensor_tensor(pi_, pi_, R, ALU.mult)
                own.do(V.tensor_tensor(kd, kd, pinv, ALU.mult), S("r_ops"))
                for p in range(PAIRS):
                    b = 4 * (p % 2)
                    dve.wait_ge(S("r_s1"), 4 * n + p + 1)
                    V.tensor_tensor(lm[:, 2 * p:2 * p + 2, :, :].rearrange("p h (m e) t -> p (h m) (e t)", e=2),
                                    ps[:, b:b + 2, :].rearrange("p h (m x) -> p (h m) x", m=2),
                                    lmask[:, d, 0:2, :].rearrange("p a b -> p (a b)").unsqueeze(1).to_broadcast([P, 4, 2 * P]), ALU.mult)
                    own.do(V.tensor_tensor(nn[:, 2 * p:2 * p + 2, 0, :], ps[:, b + 2:b + 4, 0:P],
                                           lmask[:, d, 2:3, :].to_broadcast([P, 2, P]), ALU.mult), S("r_mask"))
                for l in range(LEVELS):
                    for g in range(2):
                        dve.wait_ge(S("r_lv"), 12 * n + 2 * l + g + 1)
                        if l == 0 and g == 0:
                            dve.wait_ge(S("r_x0"), 2 * n + 2)
                        xg = xs[:, 2 * g:2 * g + 2, :, :, :].rearrange("p u k i j -> p (u k i j)")
                        own.do(V.tensor_tensor(xg, ps[:, 1 + 3 * g, :], xg, ALU.add), S("r_lvx"))
                dve.wait_ge(S("r_g"), n + 1)
                for i in range(2):
                    q = slice(64 * i, 64 * i + 64)
                    for c in range(2):
                        V.tensor_tensor(gblk[q, c, :, 64 * i:64 * i + 64],
                                        ps[q, 7 * c, :].rearrange("p (a b) -> p a b", b=P)[:, :, 64 * i:64 * i + 64],
                                        i64[q, :].unsqueeze(1).to_broadcast([64, PAIRS, HD]), ALU.add)
                dve.wait_ge(S("r_q"), n + 1)
                own.do(V.tensor_tensor(qT, ps[:, 1, :].rearrange("p (a b) -> p a b", b=P), tt[:, :, 1, :], ALU.add), S("r_gq"))
                dve.wait_ge(S("r_yl"), n + 1)
                if n >= 1:
                    own.settle()
                own.do(V.tensor_tensor(Y[:, t, :], ps[:, 5, :], Y[:, t, :], ALU.add))
                dve.wait_ge(S("r_hc"), n + 1)
                for k, c in enumerate((0, 1) if d == 0 else (1, 0)):
                    dve.wait_ge(S("r_step"), 2 * n + k + 1)
                    own.do(V.tensor_tensor(st[:, d, :, :], ps[:, 4, :].rearrange("p (a b) -> p a b", b=P), hc[:, c, :, :], ALU.add))
                    own.settle()
                    own.do(V.tensor_tensor(st[:, d, :, :], st[:, d, :, :], pc[:, :, c:c + 1].to_broadcast([P, PAIRS, P]), ALU.mult), S("r_st"))
                own.do(V.tensor_tensor(Y[:, t, :], ps[:, 6, :], Y[:, t, :], ALU.add), S("unit_ok"))
                if n == 1:
                    dve.wait_ge(S("sn_mm"), 1)
                    own.do(V.tensor_copy(sn[:, :, :, :].rearrange("p e a b -> p e (a b)"), ps[:, 2:4, :]), S("sn_ok"))
            own.settle()
            Yh = Y[:, :, :].rearrange("p t (h j) -> p (t h) j", j=HD)
            Kh = KK[:, :, :].rearrange("p t (h j) -> p (t h) j", j=HD)
            TH = NT * HEADS
            mu, var = vec["k_k"][:, 0:TH], KK[:, 0, 0:TH]
            bc = lambda v: v.unsqueeze(2).to_broadcast([P, TH, HD])
            chain = lambda i: (own.do(i), own.settle())
            chain(V.tensor_reduce(mu, Yh, AX.X, ALU.add))
            chain(V.tensor_scalar(mu, mu, 1.0 / HD, None, ALU.mult))
            chain(V.tensor_tensor(Yh, Yh, bc(mu), ALU.subtract))
            chain(V.tensor_tensor(Kh, Yh, Yh, ALU.mult))
            chain(V.tensor_reduce(mu, Kh, AX.X, ALU.add))
            own.do(V.tensor_scalar(var, mu, 1.0 / HD, GN_EPS, ALU.mult, ALU.add), S("gn_var"))
            dve.wait_ge(S("gn_rt"), 1)
            chain(V.reciprocal(mu, var))
            chain(V.tensor_tensor(Yh, Yh, bc(mu), ALU.mult))
            over = lambda v: v.unsqueeze(1).to_broadcast([P, NT, DR])
            chain(V.tensor_tensor(Y, Y, over(vec["ln_w"]), ALU.mult))
            chain(V.tensor_tensor(Y, Y, over(vec["ln_b"]), ALU.add))
            for t in range(NT):
                own.do(V.tensor_tensor(KK[:, t, :].rearrange("p (h j) -> p h j", j=HD), rkv[:, t, 2, :].rearrange("p (h j) -> p h j", j=HD),
                                       bon[:, t, :].unsqueeze(2).to_broadcast([P, HEADS, HD]), ALU.mult))
            own.settle()
            chain(V.tensor_tensor(Y, Y, KK, ALU.add))
            for t in range(NT):
                dve.wait_ge(S("g_mm"), t + 1)
                own.do(V.tensor_tensor(Y[:, t, :], Y[:, t, :], ps[:, t % 2, :], ALU.mult), S("gm_ok"))
            for i in range(2):
                dve.wait_ge(S("hid_mm"), i + 1)
                q = slice(0, HD)
                b, f = cols[q, 80 + i:81 + i], cols[q, 82 + i:83 + i]
                V.tensor_scalar(harg[q, 0, 0:LL], ps[q, 0, :], b, f, ALU.add, ALU.mult)
                own.do(V.tensor_scalar(harg[q, 0, LL:T], ps[q, 1, 0:LC], b, f, ALU.add, ALU.mult))
                own.settle()
                chain(V.tensor_scalar(harg[q, 1, :], harg[q, 0, :], 1.0 / (2 * math.pi), ROUND, ALU.mult, ALU.add))
                chain(V.tensor_scalar(harg[q, 1, :], harg[q, 1, :], ROUND, None, ALU.subtract))
                chain(V.scalar_tensor_tensor(harg[q, 2, :], harg[q, 1, :], -TWO_PI[0], harg[q, 0, :], ALU.mult, ALU.add))
                chain(V.scalar_tensor_tensor(harg[q, 2, :], harg[q, 1, :], -TWO_PI[1], harg[q, 2, :], ALU.mult, ALU.add))
                own.do(V.tensor_scalar(harg[q, 2, :], harg[q, 2, :], PI_IN, -PI_IN, ALU.min, ALU.max), S("arg_ok"))
            nf = ng = nu = ni = 0
            for tiles, _, _ in SEQS(fctx, ictx, ftab, itab):
                nk = len(tiles)
                for o in range(2):
                    if ng:
                        dve.wait_ge(S("hg_mm"), ng)
                    if nk > 1 and o == 0:
                        dve.wait_ge(S("hi_mm"), 2)
                    if nf == 0:
                        dve.wait_ge(S("sin_ok"), 2)
                    for j, t in enumerate(tiles):
                        b = 2 * (nf % 2)
                        dve.wait_ge(S("hf_mm"), nf + 1)
                        if nf:
                            own.settle()
                        V.tensor_tensor(htmp[:, 0, :], ps[:, b, :], win[:, t, :], ALU.mult)
                        chain(V.tensor_tensor(htmp[:, 1, :], ps[:, b + 1, :], win[:, t, :], ALU.mult))
                        own.do(V.tensor_tensor(yf[:, 0, j, :], htmp[:, 0, :], htmp[:, 1, :], ALU.add))
                        if j == 0:
                            own.settle()
                            own.do(V.tensor_tensor(yf[0:1, 0, 0, :], yf[0:1, 0, 0, :], hbias[0:1, DR * o:DR * o + DR], ALU.add))
                        own.do(V.tensor_tensor(yf[:, 1, j, :], htmp[:, 0, :], htmp[:, 1, :], ALU.subtract), S("hf_ok"))
                        nf += 1
                    ng += nk
                for o in range(2):
                    dve.wait_ge(S("hg_mm"), ng)
                    dve.wait_ge(S("hg_ok"), ng)
                    if ni:
                        dve.wait_ge(S("hi_mm"), ni)
                    for k in range(nk):
                        b = 2 * (nu % 2)
                        dve.wait_ge(S("hu_mm"), nu + 1)
                        own.settle()
                        gc, gs = gf[:, o, 0, k, :], gf[:, o, 1, k, :]
                        V.tensor_tensor(yf[:, 0, k, :], ps[:, b, :], gc, ALU.mult)
                        V.tensor_tensor(htmp[:, 0, :], ps[:, b + 1, :], gs, ALU.mult)
                        V.tensor_tensor(yf[:, 1, k, :], ps[:, b + 1, :], gc, ALU.mult)
                        chain(V.tensor_tensor(htmp[:, 1, :], ps[:, b, :], gs, ALU.mult))
                        V.tensor_tensor(yf[:, 0, k, :], yf[:, 0, k, :], htmp[:, 0, :], ALU.subtract)
                        own.do(V.tensor_tensor(yf[:, 1, k, :], yf[:, 1, k, :], htmp[:, 1, :], ALU.add), S("hy_ok"))
                        nu += 1
                    for t in tiles:
                        dve.wait_ge(S("hi_mm"), ni + 1)
                        own.do(V.tensor_tensor(hv[:, t, 0, :], ps[:, 4 + ni % 2, :], hv[:, t, 1 + o, :], ALU.mult), S("hz_ok"))
                        ni += 1
            dve.wait_ge(S("zsq_ok"), NT)
            own.do(V.tensor_scalar(stat[:, 40:40 + NT], stat[:, 32:32 + NT], 1.0 / DR, EPS, ALU.mult, ALU.add), S("zms_ok"))
            dve.wait_ge(S("zrt_ok"), 1)
            chain(V.reciprocal(stat[:, 56:56 + NT], stat[:, 48:48 + NT]))
            dve.wait_ge(S("ld_hn"), 16)
            for t in range(NT):
                own.do(V.scalar_tensor_tensor(hv[:, t, 0, :], hv[:, t, 0, :], stat[:, 56 + t:57 + t], hnorm, ALU.mult, ALU.mult), S("yb_ok"))
            dve.wait_ge(S("gate_ok"), 1)
            for j in range(2):
                for t in range(NT):
                    i = NT * j + t
                    dve.wait_ge(S("out_mm"), i + 1)
                    q = slice(512 * j, 512 * j + 512)
                    if i:
                        own.settle()
                    own.do(V.tensor_tensor(omul[:, i % 2, :], ps[:, 4 + i % 2, :], gbc[:, min(t, 1), q], ALU.mult))
                    own.settle()
                    own.do(V.tensor_tensor(x[:, t, q], x[:, t, q], omul[:, i % 2, :], ALU.add), S("x2_ok"))
            norm_rows(1)
            amplitude(32, 72)
            dve.wait_ge(S("ld_io"), 16)
            f3 = lambda v: v[:, :, :].rearrange("p a b -> p (a b)")

            def top_of(vals, n, width_v, width_i):
                for half in range(2):
                    o = slice(8 * half, 8 * half + 8)
                    for r in range(n):
                        m = V.max(width_v[:, r, o], vals[:, r, :])
                    chain(m)
                    for r in range(n):
                        m = V.max_index(width_i[:, r, o], width_v[:, r, o], vals[:, r, :])
                    chain(m)
                    if not half:
                        for r in range(n):
                            m = V.match_replace(vals[:, r, :], width_v[:, r, o], vals[:, r, :], -3.0e38)
                        chain(m)

            def route(t, n):
                chain(V.tensor_copy(f3(scur), sco[:, t:t + 1, :, :].rearrange("p a b c -> p (a b c)") if isinstance(t, int)
                                    else sco[:, bass.ds(t, 1), :, :].rearrange("p a b c -> p (a b c)")))
                top_of(scur, 2 * EXPH, sv, si)
                V.tensor_copy(f3(sif), f3(si))
                sv4 = sv[:, :, :].rearrange("p (h e) k -> p h e k", e=2)
                c4 = cand[:, :, :].rearrange("p h (a b) -> p h a b", b=TOPK)
                chain(V.tensor_tensor(c4, sv4[:, :, 0, :].unsqueeze(3).to_broadcast([P, EXPH, TOPK, TOPK]),
                                      sv4[:, :, 1, :].unsqueeze(2).to_broadcast([P, EXPH, TOPK, TOPK]), ALU.add))
                top_of(cand, EXPH, ts, tp)
                V.tensor_scalar(f3(ti), f3(tp), 4, None, ALU.logical_shift_right)
                chain(V.tensor_scalar(f3(tp), f3(tp), TOPK - 1, None, ALU.bitwise_and))
                sf4 = sif[:, :, :].rearrange("p (h e) k -> p h e k", e=2)
                for e, pos in ((0, ti), (1, tp)):
                    chain(V.tensor_copy(f3(tj), f3(pos)))
                    chain(V.tensor_tensor(onehot, tj[:, :, :].unsqueeze(3).to_broadcast([P, EXPH, TOPK, TOPK]),
                                          iota16.unsqueeze(1).unsqueeze(1).to_broadcast([P, EXPH, TOPK, TOPK]), ALU.is_equal))
                    chain(V.tensor_tensor(onehot, onehot, sf4[:, :, e, :].unsqueeze(2).to_broadcast([P, EXPH, TOPK, TOPK]), ALU.mult))
                    chain(V.tensor_reduce(eid[e], onehot, AX.X, ALU.add))
                chain(V.scalar_tensor_tensor(f3(eid[2]), f3(eid[0]), float(NKEY), f3(eid[1]), ALU.mult, ALU.add))
                col = (lambda v: v[:, t:t + 1, :].rearrange("p a b -> p (a b)")) if isinstance(t, int) else (lambda v: v[:, bass.ds(t, 1), :].rearrange("p a b -> p (a b)"))
                V.tensor_copy(col(eall), f3(eid[2])).then_inc(S("eid_ok"), 1)
                chain(V.tensor_copy(tsum[:, 0:EXPH], ts[:, :, 0]))
                V.tensor_tensor(ts, ts, tsum[:, 0:EXPH].unsqueeze(2).to_broadcast([P, EXPH, TOPK]), ALU.subtract).then_inc(S("top_sub"), 1)
                dve.wait_ge(S("top_exp"), n)
                chain(V.tensor_reduce(tsum[:, 0:EXPH], ts, AX.X, ALU.add))
                chain(V.reciprocal(tsum[:, EXPH:2 * EXPH], tsum[:, 0:EXPH]))
                chain(V.tensor_tensor(col(wall).rearrange("p (h k) -> p h k", k=TOPK), ts, tsum[:, EXPH:2 * EXPH].unsqueeze(2).to_broadcast([P, EXPH, TOPK]), ALU.mult))

            own.settle()
            own = rown = Own(dve, S("route_ch"))
            chain = lambda i: (rown.do(i), rown.settle())
            dve.sem_inc(S("g_used"), RING)
            dve.wait_ge(S("sc_ok"), 2 * EXPH)
            route(0, 1)
            per_route = rown.count[id(S("route_ch"))]

            def row(t, e, m):
                dve.wait_ge(row_here[m % RING], (t * (2 * SLOTS // RING) + e * (SLOTS // RING) + m // RING + 1) * 16)
                dve.wait_ge(S("g_used"), t * (2 * SLOTS) + e * SLOTS + m + RING - 1)

            def experts(t, following):
                dve.wait_ge(S("g_used"), t * (2 * SLOTS) + RING)
                V.tensor_copy(hcur, h2[:, bass.ds(t, 1), :].rearrange("p a b -> p (a b)")).then_inc(S("ex_ch"), 1)
                dve.wait_ge(S("ex_ch"), t * 4 + 1)
                V.memset(acc, 0.0).then_inc(S("ex_ch"), 1)
                dve.wait_ge(S("ex_ch"), t * 4 + 2)
                for m in range(SLOTS):
                    row(t, 0, m)
                    V.scalar_tensor_tensor(junk[:, m % 2, :], gslot[m % RING], 1.0, hcur, ALU.mult, ALU.mult,
                                           accum_out=dots[:, m:m + 1]).then_inc(S("g_used"), 1)
                if following is not None:
                    route(following, following + 1)
                dve.wait_ge(S("gelu_ok"), t + 1)
                V.tensor_tensor(coef, dots, wall[:, bass.ds(t, 1), :].rearrange("p a b -> p (a b)"), ALU.mult).then_inc(S("ex_ch"), 1)
                dve.wait_ge(S("ex_ch"), t * 4 + 3)
                for m in range(SLOTS):
                    row(t, 1, m)
                    V.scalar_tensor_tensor(acc[:, m % 2, :], gslot[m % RING], coef[:, m:m + 1], acc[:, m % 2, :],
                                           ALU.mult, ALU.add).then_inc(S("g_used"), 1)
                dve.wait_ge(S("g_used"), t * (2 * SLOTS) + 2 * SLOTS + RING)
                V.tensor_tensor(h2[:, bass.ds(t, 1), :].rearrange("p a b -> p (a b)"), acc[:, 0, :], acc[:, 1, :], ALU.add).then_inc(S("ex_ch"), 1)

            with dve.Fori(0, NT - 1) as t:
                rown.offset, rown.passed = t * per_route, S("dve_passed")
                experts(t, t + 1)
            experts(NT - 1, None)
            dve.wait_ge(S("ex_ch"), 4 * NT)
            own = Own(dve, S("fin_ch"))
            for t in range(NT):
                own.do(V.tensor_tensor(h2[:, t, :], h2[:, t, :], g2bc[:, min(t, 1), :], ALU.mult))
            own.settle()
            for t in range(NT):
                own.do(V.tensor_tensor(x[:, t, :], x[:, t, :], h2[:, t, :], ALU.add), S("x3_ok"))
            dve.wait_ge(S("fsq_ok"), NT)
            own.do(V.tensor_scalar(stat[:, 8:8 + NT], stat[:, 0:NT], 1.0 / D, EPS, ALU.mult, ALU.add), S("fms_ok"))
            dve.wait_ge(S("frt_ok"), 1)
            own.do(V.reciprocal(stat[:, 24:24 + NT], stat[:, 16:16 + NT]))
            own.settle()
            dve.wait_ge(S("ld_fn"), 16)
            for t in range(NT):
                own.do(V.scalar_tensor_tensor(x[:, t, :], x[:, t, :], stat[:, 24 + t:25 + t], fnorm, ALU.mult, ALU.mult), S("y_ok"))

        @block.gpsimd
        def _(pool):

            def gather(t):
                for e, table in ((0, a["peer_u"][0]), (1, a["peer_v"][0])):
                    for m in range(SLOTS):
                        n = t * (2 * SLOTS) + e * SLOTS + m
                        pool.wait_ge(S("g_used"), n + 1)
                        if m == 0:
                            pool.wait_ge(S("eid_ok"), t + 1)
                            pool.sem_inc(S("pool_passed"), 1)
                            pool.tensor_copy(ibuf[e], eall[:, bass.ds(t, 1), :].rearrange("p a b -> p (a b)")).then_inc(S("ib_ok"), 1)
                            pool.wait_ge(S("ib_ok"), t * 2 + e + 1)
                        pool.sem_inc(S("pool_passed"), 1)
                        pool.indirect_dma_start(gslot[m % RING], None, table, bass.IndirectOffsetOnAxis(ap=ibuf[e][:, m:m + 1], axis=0)
                                                ).then_inc(row_here[m % RING], 16)

            with pool.Fori(0, NT) as t:
                gather(t)



def small_rows(i):
    r = np.zeros((256, P), np.float32)
    r[0:48] = np.asarray(i["b_ada"])[0].reshape(48, P)
    r[48:56] = np.asarray(i["c_ctx"]).reshape(KD, P)
    r[56:64] = np.asarray(i["c"])[0].reshape(KD, P)
    r[64:72] = np.asarray(i["norm_mix"])[0].reshape(KD, P)
    r[72:80] = np.asarray(i["norm_ffn"])[0].reshape(KD, P)
    r[80, 0:64] = np.asarray(i["hy_f_b1"])[0]
    r[81, 0:64] = np.asarray(i["hy_f_b2"])[0]
    r[82:84, 0:64] = np.asarray(i["hy_freq"])[0]
    r[128:128 + 3 * NIN] = np.asarray(i["conv_w"])[0].reshape(3 * NIN, P)
    return r


OUTS = [(1, LC, D), (1, LL, D), (1, 1, 2, HEADS, HD, HD)]
RAW = ["x_prompt", "x_sample", "state_rwkv", "w_ada", "w_in", "w_out", "rwkv_w0", "rwkv_w1", "rwkv_w2", "rwkv_a0",
       "rwkv_a1", "rwkv_a2", "rwkv_g1", "rwkv_g2", "rwkv_k_k", "rwkv_k_a", "rwkv_r_k", "rwkv_ln_w", "rwkv_ln_b",
       "hy_f_w1", "hy_f_w2", "hy_f_w3", "hy_bias", "hy_norm", "peer_wq", "peer_keys", "peer_u", "peer_v", "final_norm"]


def layout(inputs):
    arrays = {n: np.ascontiguousarray(inputs[n]) for n in RAW}
    arrays["rows"] = small_rows(inputs)
    arrays["ident"] = np.eye(P, dtype=np.float32)
    i, j = np.arange(P)[:, None], np.arange(P)[None, :]
    same = i // CH == j // CH
    before = [same & (i < j), same & (i > j)]
    upto = [same & (i <= j), same & (i >= j)]
    arrays["tri"] = np.stack([np.stack([-SQD * upto[d], -SQD * before[d]], 1) for d in range(2)], 1).astype(np.float32)
    arrays["tot"] = (-SQD * (i // CH == np.arange(2)[None, :])).astype(np.float32)
    arrays["lmask"] = np.stack([np.stack([before[d], upto[d], before[1 - d]], 1) for d in range(2)], 1).astype(np.float32)
    for name, L in (("ctx", LC), ("lat", LL)):
        k, t = np.arange(L), np.arange(L)
        th = np.pi * ((2 * k[None, :] + 1) * t[:, None] % (4 * L)) / (2 * L)
        f = np.stack([np.cos(th), np.sin(th)])
        inv = np.transpose(f, (0, 2, 1)) / L
        for nm, m in (("f", f), ("i", inv)):
            m = m.reshape(2, L // P, P, L).transpose(2, 0, 1, 3).astype(np.float32)
            key = {"fctx": "fctx", "ictx": "ictx", "flat": "ftab", "ilat": "itab"}[nm + name]
            arrays[key] = np.ascontiguousarray(m[:, :, 0, :] if name == "ctx" else m)
    zs, ws = [], []
    for L in (LL, LC):
        t = np.linspace(0.0, 1.0, L, dtype=np.float32)[:, None]
        wpos = (2.0 * math.pi * np.arange(L, dtype=np.float32)[:, None] / L).astype(np.float32)
        f = np.linspace(1e-4, 7, 8, dtype=np.float32)[None, :]
        zs.append(np.concatenate([t, np.cos(f * wpos), -np.sin(f * wpos)], 1).T)
        deltas = np.linspace(math.log(1e-2) / 1.5, math.log(1e-2) / 0.3, DR, dtype=np.float32)
        ws.append(np.exp(-t * np.abs(deltas)))
    arrays["zT"] = np.ascontiguousarray(np.concatenate(zs, 1), np.float32)
    arrays["window"] = np.ascontiguousarray(np.concatenate([ws[1], ws[0]], 0).reshape(NT, P, DR).transpose(1, 0, 2), np.float32)
    arrays["iota16"] = np.tile(np.arange(TOPK, dtype=np.float32), (P, 1))
    arrays["i64"] = np.tile(np.eye(HD, dtype=np.float32), (2, 1))
    return arrays


def kernel(**inputs):
    import concourse.bacc as bacc
    from concourse.bass_utils import run_bass_kernel_spmd

    nc = bacc.Bacc("TRN2", target_bir_lowering=False, num_devices=1)
    arrays = layout(inputs)
    aps = {n: nc.dram_tensor(f"in_{n}", v.shape, mybir.dt.from_np(v.dtype), kind="ExternalInput").ap() for n, v in arrays.items()}
    outs = [nc.dram_tensor(f"out_{i}", shape, F32, kind="ExternalOutput").ap() for i, shape in enumerate(OUTS)]
    program(nc, aps, outs)
    r = run_bass_kernel_spmd(nc, [{f"in_{n}": v for n, v in arrays.items()}], core_ids=[0])
    return tuple(r.results[0][f"out_{i}"] for i in range(len(OUTS)))
```

```python
import math
from contextlib import ExitStack

import numpy as np

import concourse.bass as bass
from concourse import mybir

F32 = mybir.dt.float32
U32 = mybir.dt.uint32
ALU = mybir.AluOpType
ACT = mybir.ActivationFunctionType
AX = mybir.AxisListType

P = 128
D = 1024
KD = D // P
LC, LL = 128, 512
T = LC + LL
NT = T // P
NLT = LL // P
HD, HEADS = 64, 8
DR = HD * HEADS
PAIRS = DR // P
CH = 64
GRID = 64
NIN = 6 * DR // P
CONVROW = 80
LEVELS = 6
EXPH, TOPK, NKEY = 8, 16, 128
SLOTS = EXPH * TOPK
EPS, GN_EPS = 1e-6, 64e-5
SQD = math.exp(-0.5)
WBUF = 3
SB = 53200
RWLOADS = 13
UNITS = [(0, 0), (0, 1)] + [u for i in range(NLT) for u in ((1 + i, 0), (NLT - i, 1))]


class Own:

    def __init__(self, eng, chain):
        self.eng, self.chain, self.count, self.last, self.offset, self.passed = eng, chain, {}, None, 0, None

    def do(self, ins, sem=None):
        sem = sem or self.chain
        ins.then_inc(sem, 1)
        self.count[id(sem)] = self.count.get(id(sem), 0) + 1
        self.last = (sem, self.count[id(sem)])

    def settle(self):
        if isinstance(self.offset, int):
            self.eng.wait_ge(self.last[0], self.last[1] + self.offset)
        else:
            self.eng.wait_ge(self.last[0], self.last[1] + self.offset)
            self.eng.sem_inc(self.passed, 1)


RING = 16
EARLY = 4
ROUTE_ROWS = (100, 122)
OUT_ORDER = [(0, 0), (0, 1)] + [(t, j) for j in range(2) for t in range(1, NT)]
QORDER = list(range(2 * EXPH)) + [4 * j + f for j in (3, 1, 2, 0) for f in range(4)]
ROUND = 1.5 * 2.0 ** 23
TWO_PI = (6.28125, 2 * math.pi - 6.28125)
PI_IN = 3.1415925


def SEQS(fctx, ictx, ftab, itab):
    yield [0], fctx[:, :, :].unsqueeze(2), ictx[:, :, :].unsqueeze(2)
    yield [1, 2, 3, 4], ftab, itab


PREP_PE = (1, 3, 7, 8, 9, 10, 11)
PREP_ACT = {0: 1, 1: 1, 4: 1, 5: 2, 6: 1, 8: 1, 9: 2, 10: 1}
PREP_DVE = {0: 2, 3: 2, 4: 3, 5: 2, 6: 1}


def weight_chunks():
    order = [("ada", j) for j in range(4)]
    for j in range(6):
        order += [("in", j)] + [("ada", 4 + 2 * j + i) for i in range(2) if j < 4]
    return order + [("out", j) for j in range(2)] + [("wq", j) for j in range(4)] + [("wq again", 0)]


def program(nc, a, outs):
    y_prompt, y_sample, new_state = outs
    WCH = weight_chunks()
    slot_of = {w: n % WBUF for n, w in enumerate(WCH)}
    turn_of = {w: n // WBUF for n, w in enumerate(WCH)}

    with ExitStack() as ctx:
        def sem(name):
            return ctx.enter_context(nc.semaphore(name))

        arena = ctx.enter_context(nc.sbuf_tensor("arena", [P, SB], F32))
        ps = ctx.enter_context(nc.psum_tensor("ps", [P, 8, 512], F32))

        def at(off, *shape):
            n = int(np.prod(shape))
            v = arena[:, off:off + n]
            if len(shape) == 2:
                v = v.rearrange("p (a b) -> p a b", b=shape[1])
            elif len(shape) == 3:
                v = v.rearrange("p (a b c) -> p a b c", b=shape[1], c=shape[2])
            elif len(shape) == 4:
                v = v.rearrange("p (a b c d) -> p a b c d", b=shape[1], c=shape[2], d=shape[3])
            return v

        class Region:
            def __init__(self, start, end):
                self.at_, self.end = start, end

            def __call__(self, *shape):
                v = at(self.at_, *shape)
                self.at_ += int(np.prod(shape))
                assert self.at_ <= self.end, (self.at_, self.end)
                return v

        keep = Region(0, 23000)
        ident = keep(P)
        x = keep(NT, D)
        hT = keep(KD, T)
        cols = keep(P)
        colsB = keep(P)
        csil = keep(2, KD)
        mod = keep(48, 2)
        amp = keep(KD, 2)
        stat = keep(64)
        hv = keep(NT, 3, DR)
        epsc = keep(4)
        w_end = keep.at_
        rw = Region(w_end, SB)
        rkv = rw(NT, 3, DR)
        KK = rw(NT, DR)
        Y = rw(NT, DR)
        yT = at(rw.at_ - 2 * NT * DR, 2, 4, T)
        bon = rw(NT, HEADS)
        tanhT, aloT, gateT = rw(T), rw(T), rw(T)
        vec = {n: rw(DR) for n in ("k_k", "k_a", "ln_w", "ln_b")}
        vec.update({n: rw(2, DR) for n in ("w0", "a0", "r_k")})
        lora1 = at(rw.at_ - 5 * 2 * DR, KD, 3 * P)
        sc = Region(rw.at_, SB)
        lm = at(ident.offset + P + NT * D, HEADS, 4, P)
        nn = sc(HEADS, 2, P)
        xs = sc(PAIRS, 2, 2, HD)
        xr = Region(x.offset, x.offset + NT * D)
        tt2 = [sc(PAIRS, 4, P), xr(PAIRS, 4, P)]
        wsg, av, pi_, pinv, pex = (sc(DR) for _ in range(5))
        kd2, bt2 = ([sc(DR), xr(DR)] for _ in range(2))
        gblk = sc(2, PAIRS, P)
        hc = sc(2, PAIRS, P)
        qT = sc(PAIRS, P)
        st2 = [sc(2, PAIRS, P), xr(2, PAIRS, P)]
        sn = sc(2, PAIRS, P)
        pc2 = [sc(PAIRS, 2), xr(PAIRS, 2)]
        hn = sc(4 * HEADS)
        tri = sc(2, 2, P)
        tot = sc(2)
        lmask = sc(2, 3, P)
        w2, a2 = (at(ident.offset + P + NT * D + 4096 + i * DR, DR) for i in range(2))
        i64 = sc(HD)
        g2 = at(rw.at_, DR)
        hy = Region(w_end, rw.at_)
        gf = hy(2, 2, 4, DR)
        yf = hy(2, 4, DR)
        win = hy(NT, DR)
        hid = hy(T)
        fw1, fw2 = hy(HD), hy(HD)
        fw3 = hy(4 * DR)
        htmp = hy(2, DR)
        fctx, ictx = hy(2, P), hy(2, P)
        zT = at(yf.offset, T)
        harg = at(yf.offset + T, 3, T)
        hnorm = at(win.offset, DR)
        gbc = at(gf.offset, 2, D)
        omul = at(gf.offset + 2 * D, 2, DR)
        pr = Region(w_end, rw.at_ + 2600)
        h2 = pr(NT, D)
        sco = pr(NT, 2 * EXPH, NKEY)
        qbuf = pr(2, T)
        keyT = pr(2 * EXPH, NKEY)
        eall = pr(NT, SLOTS).bitcast(U32)
        wall = pr(NT, SLOTS)
        g2bc = pr(2, D)
        assert pr.at_ <= SB - WBUF * KD * 512
        xn2 = at(sco.offset + 2 * EXPH * NKEY * NT - NT * D, NT, D)
        tk = Region(hv.offset, hv.offset + NT * 3 * DR)
        scur = tk(2 * EXPH, NKEY)
        cand = tk(EXPH, TOPK * TOPK)
        sv = tk(2 * EXPH, TOPK)
        si = tk(2 * EXPH, TOPK).bitcast(U32)
        sif = tk(2 * EXPH, TOPK)
        ts, tp, ti, tj, tf = (tk(EXPH, TOPK) for _ in range(5))
        tp, ti = tp.bitcast(U32), ti.bitcast(U32)
        eid = [tk(EXPH, TOPK) for _ in range(3)]
        iota16 = tk(TOPK)
        dots = tk(SLOTS)
        coef = tk(SLOTS)
        ibuf = [tk(SLOTS).bitcast(U32) for _ in range(2)]
        tsum = tk(2 * EXPH)
        onehot = at(scur.offset, EXPH, TOPK, TOPK)
        hbias = at(rw.at_ + DR, 2 * DR)[0:1, :]
        keyN = at(hv.offset, 2 * EXPH, NKEY)
        ring_at = SB - WBUF * KD * 512
        ring = [at(ring_at + i * KD * 512, KD, 512) for i in range(WBUF)]
        assert rw.at_ <= ring_at
        ftab = at(ring_at + KD * 512, 2, 4, DR)
        itab = at(ring_at + 2 * KD * 512, 2, 4, DR)
        hT_at = ident.offset + P + NT * D
        gslot = ([at(ring_at + i * D, D) for i in range(8)] + [at(hT_at + 4 * D, D)] + [at(qbuf.offset + i * D, D) for i in range(3)]
                 + [at(ring_at + (8 + i) * D, D) for i in range(EARLY)])
        hcur = at(hT_at, D)
        acc = at(hT_at + D, 2, D)
        junk = tk(D).bitcast(mybir.dt.bfloat16).rearrange("p (a b) -> p a b", b=D)
        fnorm = at(sco.offset, D)
        sqj = at(sco.offset + D, NT, D)
        xn = at(w_end, NT, D)

        s = {}

        def S(name):
            if name not in s:
                s[name] = sem(name)
            return s[name]

        for n in ("ld_x", "ld_small", "ld_lora", "ld_vec", "pe_ch", "dve_ch", "act_ch", "pool_ch",
                  "rows_T", "cols_ok", "sig_c", "csil_ok", "ada_mm", "mod_ok", "sq_ok", "ms_ok", "rt_ok", "xn_ok",
                  "amp_ok", "xT_mm", "hT_ok", "in_mm", "conv_mid", "conv_ok", "uT_mm", "u_ok", "lora_mm", "lora_ok", "out_done"):
            S(n)
        row_here = [sem(f"row_here{i}") for i in range(RING)]
        first_here = [sem(f"first_here{i}") for i in range(EARLY)]
        wl = [sem(f"w_loaded{i}") for i in range(WBUF)]

        def w_free(eng, w):
            kind, j = w
            eng.wait_ge(*{"ada": (S("ada_mm"), j + 1), "in": (S("in_mm"), 4 * j + 4),
                          "out": (S("out_mm"), NT + 1 if j == 0 else 2 * NT), "wq": (S("q_mm"), 4 * j + 4)}[kind])

        def w_wait(eng, w):
            eng.wait_ge(wl[slot_of[w]], 16 * (turn_of[w] + 1))

        block = ctx.enter_context(nc.Block())

        @block.sync
        def _(sp):
            sp.dma_start(x[:, 0, :], a["x_prompt"][0]).then_inc(S("ld_x"), 16)
            sp.dma_start(cols, a["rows"][0:128, :]).then_inc(S("ld_small"), 16)
            sp.dma_start(colsB, a["rows"][128:256, :]).then_inc(S("ld_small"), 16)
            sp.dma_start(ident, a["ident"]).then_inc(S("ld_small"), 16)
            sp.dma_start(x[:, 1:NT, :], a["x_sample"][0].rearrange("(t p) d -> p t d", p=P)).then_inc(S("ld_x"), 16)
            src = {"ada": a["w_ada"], "in": a["w_in"], "out": a["w_out"], "wq": a["peer_wq"]}
            for n, (kind, j) in enumerate(WCH):
                if kind == "out":
                    break
                if n == 2:
                    for d in range(2):
                        sp.dma_start(lora1[:, :, 64 * d:64 * d + 64], a["rwkv_w1"][0, d].rearrange("(k p) n -> p k n", p=P)).then_inc(S("ld_lora"), 16)
                        sp.dma_start(lora1[:, :, 128 + 64 * d:192 + 64 * d], a["rwkv_a1"][0, d].rearrange("(k p) n -> p k n", p=P)).then_inc(S("ld_lora"), 16)
                    sp.dma_start(lora1[:, :, 256:384], a["rwkv_g1"][0].rearrange("(k p) n -> p k n", p=P)).then_inc(S("ld_lora"), 16)
                if n >= WBUF and n < 18:
                    w_free(sp, WCH[n - WBUF])
                w = src[kind][0, :, 512 * j:512 * j + 512].rearrange("(k p) n -> p k n", p=P)
                sp.dma_start(ring[n % WBUF], w).then_inc(wl[n % WBUF], 16)
            sp.wait_ge(S("lora_mm"), 3)
            ld = S("ld_rw")
            for nm in ("k_k", "k_a", "ln_w", "ln_b"):
                sp.dma_start(vec[nm], a["rwkv_" + nm][0].partition_broadcast(P)).then_inc(ld, 16)
            for nm in ("w0", "a0"):
                sp.dma_start(vec[nm], a["rwkv_" + nm][0].partition_broadcast(P)).then_inc(ld, 16)
            sp.dma_start(vec["r_k"], a["rwkv_r_k"][0].rearrange("d h j -> d (h j)").partition_broadcast(P)).then_inc(ld, 16)
            for dst, nm in ((w2, "rwkv_w2"), (a2, "rwkv_a2")):
                sp.dma_start(dst, a[nm][0].rearrange("d k n -> (d k) n")).then_inc(ld, 16)
            sp.dma_start(tri, a["tri"]).then_inc(ld, 16)
            sp.dma_start(tot, a["tot"]).then_inc(ld, 16)
            sp.dma_start(lmask, a["lmask"]).then_inc(ld, 16)
            sp.dma_start(i64, a["i64"]).then_inc(ld, 16)
            sp.wait_ge(S("sn_zero"), 1)
            for d in range(2):
                for h in range(HEADS):
                    i, p = h % 2, h // 2
                    sp.dma_start(sn[64 * i:64 * i + 64, d, p, 64 * i:64 * i + 64], a["state_rwkv"][0, 0, d, h]).then_inc(S("sn_in"), 16)
            sp.wait_ge(S("sn_ok"), 1)
            for d in range(2):
                for h in range(HEADS):
                    i, p = h % 2, h // 2
                    sp.dma_start(new_state[0, 0, d, h], sn[64 * i:64 * i + 64, d, p, 64 * i:64 * i + 64]).then_inc(S("out_state"), 16)
            sp.wait_ge(S("out_state"), 16 * 16)
            sp.wait_ge(S("unit_ok"), len(UNITS))
            sp.dma_start(g2, a["rwkv_g2"][0]).then_inc(S("ld_g2"), 16)
            sp.dma_start(x[:, 0, :], a["x_prompt"][0]).then_inc(S("ld_x"), 16)
            sp.dma_start(x[:, 1:NT, :], a["x_sample"][0].rearrange("(t p) d -> p t d", p=P)).then_inc(S("ld_x"), 16)
            sp.dma_start(itab, a["itab"]).then_inc(S("ld_tab"), 16)
            sp.dma_start(ftab, a["ftab"]).then_inc(S("ld_tab"), 16)

            def load_w(n):
                kind, j = WCH[n]
                sp.dma_start(ring[n % WBUF], src[kind.split()[0]][0, :, 512 * j:512 * j + 512].rearrange("(k p) n -> p k n", p=P)).then_inc(wl[n % WBUF], 16)

            load_w(18)
            sp.wait_ge(S("ya_T"), 4)
            for dst, srcv in ((win, a["window"]), (zT[0:17, :], a["zT"]), (fw1[0:17, :], a["hy_f_w1"][0]), (fw2[0:64, :], a["hy_f_w2"][0]),
                              (fw3[0:64, :], a["hy_f_w3"][0]), (fctx, a["fctx"]), (ictx, a["ictx"])):
                sp.dma_start(dst, srcv).then_inc(S("ld_hy"), 16)
            sp.dma_start(hbias[:, :], a["hy_bias"][0].rearrange("o n -> (o n)").unsqueeze(0)).then_inc(S("ld_hy"), 16)
            sp.wait_ge(S("hf_ok"), 2 * NT)
            sp.dma_start(hnorm, a["hy_norm"][0].partition_broadcast(P)).then_inc(S("ld_hn"), 16)
            sp.wait_ge(S("hu_mm"), 2 * 5)
            load_w(19)
            sp.wait_ge(S("hi_mm"), 2 * 5)
            load_w(20)
            sp.wait_ge(S("yb_T"), 4)
            sp.dma_start(keyN, a["peer_keys"][0].rearrange("e h k d -> k (e h) d")).then_inc(S("ld_key"), 16)
            sp.dma_start(iota16, a["iota16"]).then_inc(S("ld_io"), 16)
            w_free(sp, WCH[18])
            load_w(21)
            w_free(sp, WCH[19])
            load_w(22)
            w_free(sp, WCH[20])
            load_w(23)
            sp.wait_ge(S("q_mm"), 24)
            load_w(24)
            sp.wait_ge(S("x3_ok"), NT)
            sp.dma_start(fnorm, a["final_norm"].partition_broadcast(P)).then_inc(S("ld_fn"), 16)
            sp.wait_ge(S("y_ok"), NT)
            sp.dma_start(y_prompt[0], x[:, 0, :]).then_inc(S("out_y"), 16)
            sp.dma_start(y_sample[0].rearrange("(t p) d -> p t d", p=P), x[:, 1:NT, :]).then_inc(S("out_y"), 16)
            sp.wait_ge(S("out_y"), 32)

        @block.tensor
        def _(pe):
            pe.wait_ge(S("ld_small"), 48)
            pe.transpose(ps[:, 0, 0:P], cols, ident)
            pe.transpose(ps[:, 0, P:2 * P], colsB, ident).then_inc(S("rows_T"), 1)

            def ada(j):
                w_wait(pe, ("ada", j))
                if j >= 2:
                    pe.wait_ge(S("mod_ok"), j - 1)
                for f in range(4):
                    o = ps[:, 6 + j % 2, 2 * f:2 * f + 2]
                    for k in range(KD):
                        m = pe.matmul(o, ring[slot_of["ada", j]][:, k, P * f:P * f + P], csil[:, :, k],
                                      start=(k == 0), stop=(k == KD - 1))
                m.then_inc(S("ada_mm"), 1)

            pe.wait_ge(S("csil_ok"), 1)
            for j in range(4):
                ada(j)

            def norm_T(first):
                pe.wait_ge(S("xn_ok"), first + 1)
                for k in range(KD):
                    n = first * KD + k
                    if n >= 3:
                        pe.wait_ge(S("hT_ok"), n - 2)
                    for t in range(NLT):
                        pe.transpose(ps[:, k % 3, P * t:P * t + P], xn[:, 1 + t, P * k:P * k + P], ident)
                    pe.transpose(ps[:, 3 + k % 3, 0:P], xn[:, 0, P * k:P * k + P], ident).then_inc(S("xT_mm"), 1)

            norm_T(0)
            pe.wait_ge(S("hT_ok"), KD)

            def to_rows(c):
                pe.wait_ge(S("conv_ok"), 4 * c + 4)
                for t in range(NT):
                    i = NT * c + t
                    if i >= 2:
                        pe.wait_ge(S("u_ok"), i - 1)
                    for f in range(4):
                        m = pe.transpose(ps[:, 4 + i % 2, P * f:P * f + P], yT[:, c % 2, f, P * t:P * t + P], ident)
                    m.then_inc(S("uT_mm"), 1)

            for n in range(NIN):
                c, f = divmod(n, 4)
                if f == 0:
                    w_wait(pe, ("in", c))
                if n >= 2:
                    pe.wait_ge(S("conv_ok"), n - 1)
                w = ring[slot_of["in", c]]
                for k in range(KD):
                    pe.matmul(ps[:, n % 2, :], w[:, k, P * f:P * f + P], hT[:, k, LC:T], start=(k == 0), stop=(k == KD - 1))
                for k in range(KD):
                    m = pe.matmul(ps[:, 2 + n % 2, 0:LC], w[:, k, P * f:P * f + P], hT[:, k, 0:LC], start=(k == 0), stop=(k == KD - 1))
                m.then_inc(S("in_mm"), 1)
                if f == 3 and c < 4:
                    ada(4 + 2 * c)
                    ada(5 + 2 * c)
                if f == 1 and c >= 1:
                    to_rows(c - 1)
            to_rows(5)
            pe.wait_ge(S("ld_lora"), 80)
            for i, (bl, bc) in enumerate(((0, 2), (1, 3), (4, 5))):
                if i == 0:
                    pe.wait_ge(S("conv_ok"), NIN)
                if i == 2:
                    pe.wait_ge(S("u_ok"), 6 * NT)
                for k in range(KD):
                    pe.matmul(ps[:, bl, :], lora1[:, k, P * i:P * i + P], hT[:, k, LC:T], start=(k == 0), stop=(k == KD - 1))
                for k in range(KD):
                    m = pe.matmul(ps[:, bc, 0:LC], lora1[:, k, P * i:P * i + P], hT[:, k, 0:LC], start=(k == 0), stop=(k == KD - 1))
                m.then_inc(S("lora_mm"), 1)
            pe.wait_ge(S("ld_rw"), 16 * RWLOADS)
            pe.wait_ge(S("lora_ok"), 3)
            pe.wait_ge(S("sn_in"), 16 * 16)
            for e in range(2):
                for p in range(PAIRS):
                    m = pe.transpose(ps[:, 2 + e, P * p:P * p + P], sn[:, e, p, :], ident)
            m.then_inc(S("st_mm"), 1)
            pe.wait_ge(S("st_in"), 1)

            def prepare(n):
                if n >= len(UNITS):
                    while True:
                        yield
                t, d = UNITS[n]
                pe.matmul(ps[:, 0, :], tanhT[64 * d:64 * d + 64, P * t:P * t + P], w2[64 * d:64 * d + 64, :], start=True, stop=True)
                pe.matmul(ps[:, 7, :], aloT[64 * d:64 * d + 64, P * t:P * t + P], a2[64 * d:64 * d + 64, :], start=True, stop=True).then_inc(S("r_lora"), 1)
                yield
                pe.wait_ge(S("r_sig"), 2 * n + 2)
                pe.matmul(ps[:, 0, :], tri[:, d, 0, :], wsg, start=True, stop=True)
                pe.matmul(ps[:, 7, :], tri[:, d, 1, :], wsg, start=True, stop=True).then_inc(S("r_cum"), 1)
                yield
                pe.wait_ge(S("r_exp"), 4 * n + 3)
                for p in range(PAIRS):
                    m = pe.matmul(ps[:, 0, 2 * p:2 * p + 2], wsg[:, P * p:P * p + P], tot, start=True, stop=True)
                m.then_inc(S("r_cum"), 1)
                yield
                pe.wait_ge(S("r_ops"), n + 1)
                pe.wait_ge(S("r_exp"), 4 * n + 4)
                for p in range(PAIRS):
                    if p >= 2:
                        pe.wait_ge(S("r_tt"), 4 * n + p - 1)
                    for i, v in enumerate((pex, pi_, bt2[n % 2], kd2[n % 2])):
                        m = pe.transpose(ps[:, 7 * (p % 2), P * i:P * i + P], v[:, P * p:P * p + P], ident)
                    m.then_inc(S("r_tr"), 1)
                    yield
                while True:
                    yield

            def products(n, p):
                tt = tt2[n % 2]
                pe.wait_ge(S("r_tt"), 4 * n + 4)
                if p >= 2:
                    pe.wait_ge(S("r_mask"), 4 * n + p - 1)
                b = 4 * (p % 2)
                for i in range(2):
                    q = slice(64 * i, 64 * i + 64)
                    ar = tt[q, p, 0:2, :]
                    pe.matmul(ps[:, b + i, 0:256], tt[q, p, 2, :], ar, start=True, stop=True)
                    pe.matmul(ps[:, b + i, 256:512], tt[q, p, 3, :], ar, start=True, stop=True)
                    m = pe.matmul(ps[:, b + 2 + i, 0:P], tt[q, p, 0, :], tt[q, p, 2, :], start=True, stop=True)
                m.then_inc(S("r_s1"), 1)

            first = prepare(0)
            for _ in range(7):
                next(first)
            products(0, 0)
            products(0, 1)
            for n, (t, d) in enumerate(UNITS):
                kd, bt, st = kd2[n % 2], bt2[n % 2], st2[min(t, 1)]
                products(n, 2)
                products(n, 3)
                pe.wait_ge(S("r_mask"), 4 * n + 4)
                for h in range(HEADS):
                    m = pe.matmul(ps[:, 0, 64 * h:64 * h + 64], lm[:, h, 2, :], rkv[:, t, 2, 64 * h:64 * h + 64], start=True, stop=True)
                m.then_inc(S("r_s2"), 1)
                ahead = prepare(n + 1)
                for l in range(LEVELS):
                    for g in range(2):
                        if l == 0:
                            pe.wait_ge(S("r_x0"), 2 * n + 2)
                        else:
                            pe.wait_ge(S("r_lvx"), 12 * n + 2 * (l - 1) + g + 1)
                            pe.wait_ge(S("r_lvn"), 10 * n + 2 * (l - 1) + g + 1)
                        for j in range(4):
                            h = 4 * g + j
                            nT = lm[:, h, 0, :] if l == 0 else nn[:, h, 1, :]
                            q = slice(P * j, P * j + P)
                            m = pe.matmul(ps[:, 1 + 3 * g, :].rearrange("p (u k i j) -> p u k i j", u=2, k=2, i=2)[:, j // 2, :, j % 2, :], nT,
                                          xs[:, h // 2, :, h % 2, :], start=True, stop=True)
                            if l < LEVELS - 1:
                                pe.matmul(ps[:, 2 + 3 * g, q], nT, nn[:, h, 0, :], start=True, stop=True)
                                m = pe.matmul(ps[:, 3 + 3 * g, q], nn[:, h, 0, :], nT, start=True, stop=True)
                        m.then_inc(S("r_lv"), 1)
                        if 2 * l + g in PREP_PE:
                            next(ahead)
                pe.wait_ge(S("r_lvx"), 12 * n + 12)
                pe.wait_ge(S("r_lvn"), 10 * n + 10)
                if n + 1 < len(UNITS):
                    pe.wait_ge(S("r_tt"), 4 * n + 8)
                for p in range(PAIRS):
                    f = slice(P * p, P * p + P)
                    for c in range(2):
                        q = slice(64 * c, 64 * c + 64)
                        m = pe.matmul(ps[:, 7 * c, f], xs[q, p, 0, :, :].rearrange("p a b -> p (a b)"), bt[q, f], start=True, stop=True)
                m.then_inc(S("r_g"), 1)
                for h in range(HEADS):
                    i, p = h % 2, h // 2
                    m = pe.matmul(ps[64 * i:64 * i + 64, 1, P * p:P * p + P], xs[:, p, 0, i, :], lm[:, h, 1, :], start=True, stop=True)
                m.then_inc(S("r_q"), 1)
                for p in range(PAIRS):
                    f = slice(P * p, P * p + P)
                    for c in range(2):
                        q = slice(64 * c, 64 * c + 64)
                        pe.matmul(ps[:, 2 + c, f], kd[q, f], rkv[q, t, 2, f], start=True, stop=False)
                        m = pe.matmul(ps[:, 2 + c, f], bt[q, f], xs[q, p, 1, :, :].rearrange("p a b -> p (a b)"), start=False, stop=True)
                m.then_inc(S("r_hm"), 1)
                for h in range(HEADS):
                    f = slice(64 * h, 64 * h + 64)
                    pe.matmul(ps[:, 5, f], lm[:, h, 3, :], rkv[:, t, 2, f], start=True, stop=False)
                    m = pe.matmul(ps[:, 5, f], lm[:, h, 1, :], xs[:, h // 2, 1, h % 2, :], start=False, stop=True)
                m.then_inc(S("r_yl"), 1)
                pe.wait_ge(S("r_gq"), n + 1)
                for k, c in enumerate((0, 1) if d == 0 else (1, 0)):
                    if n >= 1 or k:
                        pe.wait_ge(S("r_st"), 2 * n + k)
                    for p in range(PAIRS):
                        f = slice(P * p, P * p + P)
                        m = pe.matmul(ps[:, 4, f], gblk[:, c, p, :], st[:, d, p, :], start=True, stop=True)
                    for p in range(PAIRS):
                        m = pe.matmul(ps[64 * c:64 * c + 64, 6, P * p:P * p + P], qT[:, p, 64 * c:64 * c + 64], st[:, d, p, :], start=True, stop=True)
                    m.then_inc(S("r_step"), 1)
                    if k == 0 and n + 1 < len(UNITS):
                        pe.wait_ge(S("r_hc"), n + 1)
                        products(n + 1, 0)
                pe.wait_ge(S("unit_ok"), n + 1)
                if n == 1:
                    for e in range(2):
                        for p in range(PAIRS):
                            m = pe.transpose(ps[:, 4 + e, P * p:P * p + P], st[:, e, p, :], ident)
                    m.then_inc(S("sn_mm"), 1)
                    pe.wait_ge(S("sn_ok"), 1)
                if n + 1 < len(UNITS):
                    products(n + 1, 1)
            pe.wait_ge(S("unit_ok"), len(UNITS))
            pe.wait_ge(S("ld_g2"), 16)
            for t in range(NT):
                if t >= 2:
                    pe.wait_ge(S("gm_ok"), t - 1)
                pe.matmul(ps[:, t % 2, :], gateT[:, P * t:P * t + P], g2, start=True, stop=True).then_inc(S("g_mm"), 1)

            def mix_T(which, ok):
                for k in range(4):
                    if k == 0:
                        pe.wait_ge(ok, NT)
                    if k >= 2:
                        pe.wait_ge(S("mix_ok"), 4 * which + k - 1)
                    elif which:
                        pe.wait_ge(S("mix_ok"), 4)
                    for t in range(NT):
                        v = hv[:, t, 0, P * k:P * k + P] if which else Y[:, t, P * k:P * k + P]
                        b = (2 + 2 * (k % 2), P * (t - 1)) if t else (3 + 2 * (k % 2), 0)
                        m = pe.transpose(ps[:, b[0], b[1]:b[1] + P], v, ident)
                    m.then_inc(S("yb_T" if which else "ya_T"), 1)

            mix_T(0, S("gm_ok"))
            pe.wait_ge(S("ld_hy"), 8 * 16)
            pe.wait_ge(S("gm_ok"), NT)
            pe.wait_ge(S("mix_ok"), 4)
            pe.matmul(ps[0:HD, 0, :], fw1[0:17, :], zT[0:17, 0:LL], start=True, stop=True)
            pe.matmul(ps[0:HD, 1, 0:LC], fw1[0:17, :], zT[0:17, LL:T], start=True, stop=True).then_inc(S("hid_mm"), 1)
            pe.wait_ge(S("sin_ok"), 1)
            pe.matmul(ps[0:HD, 0, :], fw2[0:HD, :], hid[0:HD, 0:LL], start=True, stop=True)
            pe.matmul(ps[0:HD, 1, 0:LC], fw2[0:HD, :], hid[0:HD, LL:T], start=True, stop=True).then_inc(S("hid_mm"), 1)
            pe.wait_ge(S("sin_ok"), 2)
            pe.wait_ge(S("ld_tab"), 32)
            nf = ng = nu = ni = 0
            for tiles, fcs, ics in SEQS(fctx, ictx, ftab, itab):
                nk = len(tiles)
                for o in range(2):
                    for t in tiles:
                        b = 2 * (nf % 2)
                        if nf >= 2:
                            pe.wait_ge(S("hf_ok"), nf - 1)
                        pos = slice(LL, T) if t == 0 else slice(P * (t - 1), P * t)
                        for e in range(2):
                            q = slice(DR * (2 * o + e), DR * (2 * o + e) + DR)
                            m = pe.matmul(ps[:, b + e, :], hid[0:HD, pos], fw3[0:HD, q], start=True, stop=True)
                        m.then_inc(S("hf_mm"), 1)
                        nf += 1
                    pe.wait_ge(S("hf_ok"), nf)
                    for k in range(nk):
                        b = 4 + 2 * (ng % 2)
                        if ng >= 2:
                            pe.wait_ge(S("hg_ok"), ng - 1)
                        for e in range(2):
                            for j in range(nk):
                                m = pe.matmul(ps[:, b + e, :], fcs[:, e, j, P * k:P * k + P], yf[:, e, j, :], start=(j == 0), stop=(j == nk - 1))
                        m.then_inc(S("hg_mm"), 1)
                        ng += 1
                for o in range(2):
                    if o:
                        pe.wait_ge(S("hz_ok"), ni)
                    pe.wait_ge(S("hg_ok"), ng)
                    for k in range(nk):
                        b = 2 * (nu % 2)
                        if nu >= 2:
                            pe.wait_ge(S("hy_ok"), nu - 1)
                        for e in range(2):
                            for j, t in enumerate(tiles):
                                m = pe.matmul(ps[:, b + e, :], fcs[:, e, j, P * k:P * k + P], hv[:, t, 0, :], start=(j == 0), stop=(j == nk - 1))
                        m.then_inc(S("hu_mm"), 1)
                        nu += 1
                    pe.wait_ge(S("hy_ok"), nu)
                    for j in range(nk):
                        if ni >= 2:
                            pe.wait_ge(S("hz_ok"), ni - 1)
                        for e in range(2):
                            for k in range(nk):
                                m = pe.matmul(ps[:, 4 + ni % 2, :], ics[:, e, k, P * j:P * j + P], yf[:, e, k, :],
                                              start=(e == 0 and k == 0), stop=(e == 1 and k == nk - 1))
                        m.then_inc(S("hi_mm"), 1)
                        ni += 1
            pe.wait_ge(S("hz_ok"), ni)

            def spread(first, src_col, bank):
                for c in range(2):
                    for k in range(KD):
                        m = pe.matmul(ps[:, bank + 2 * c + k // 4, P * (k % 4):P * (k % 4) + P],
                                      mod[:, src_col + k, c:c + 1].to_broadcast([P, P]), ident, start=True, stop=True)
                m.then_inc(S("gate_mm"), 1)

            mix_T(1, S("yb_ok"))
            pe.wait_ge(S("mix_ok"), 8)
            pe.wait_ge(S("mod_ok"), 12)
            spread(0, 16, 0)
            pe.wait_ge(S("gate_ok"), 1)
            for i, (t, j) in enumerate(OUT_ORDER):
                w_wait(pe, ("out", j))
                if i >= 2:
                    pe.wait_ge(S("x2_ok"), i - 1)
                for k in range(KD):
                    m = pe.matmul(ps[:, 4 + i % 2, :], hT[:, k, P * t:P * t + P], ring[slot_of["out", j]][:, k, :], start=(k == 0), stop=(k == KD - 1))
                m.then_inc(S("out_mm"), 1)
                if i == 3:
                    pe.wait_ge(S("n2_xn"), 1)
                    for k in range(KD):
                        m = pe.transpose(ps[:, 6 + k // 4, P * (k % 4):P * (k % 4) + P], xn2[:, 0, P * k:P * k + P], ident)
                        if k % 4 == 3:
                            m.then_inc(S("n2_T"), 1)
            pe.wait_ge(S("ld_key"), 16)
            for g in range(4):
                for i in range(4):
                    hh = 4 * g + i
                    m = pe.transpose(ps[:, g, P * i:P * i + P], keyN[:, EXPH * (hh % 2) + hh // 2, :], ident)
                m.then_inc(S("key_mm"), 1)
            pe.wait_ge(S("key_ok"), 4)
            pe.wait_ge(S("h2T_ok"), KD)

            def latent_input():
                pe.wait_ge(S("n2_xn"), 2)
                for k in range(KD):
                    if k >= 2:
                        pe.wait_ge(S("h2T_ok"), KD + k - 1)
                    for t in range(NLT):
                        m = pe.transpose(ps[:, k % 2, P * t:P * t + P], xn2[:, 1 + t, P * k:P * k + P], ident)
                    m.then_inc(S("n2_T"), 1)
                pe.wait_ge(S("x2_ok"), 2 * NT)
                pe.wait_ge(S("h2T_ok"), 2 * KD)
                for t in range(NT):
                    for g in range(2):
                        i = 2 * t + g
                        if i >= 2:
                            pe.wait_ge(S("h2_ok"), i - 1)
                        for k in range(4 * g, 4 * g + 4):
                            m = pe.transpose(ps[:, 4 + i % 2, P * (k % 4):P * (k % 4) + P], hT[:, k, P * t:P * t + P], ident)
                        m.then_inc(S("h2_mm"), 1)
                spread(1, 40, 0)
                pe.wait_ge(S("gate_ok"), 2)

            def scores(i):
                n = QORDER[i]
                pe.wait_ge(S("q_ok"), i + 1)
                if i >= 1:
                    pe.wait_ge(S("sc_ok"), i)
                for t in ([0] if i < 2 * EXPH else range(1, NT)):
                    b = (6, P * (t - 1)) if t else (7, 0)
                    m = pe.matmul(ps[:, b[0], b[1]:b[1] + P], qbuf[:, i % 2, P * t:P * t + P], keyT[:, n, :], start=True, stop=True)
                m.then_inc(S("sc_mm"), 1)

            for i, n in enumerate(QORDER):
                j, f = divmod(n, 4)
                again = i >= 2 * EXPH
                if i == 2 * EXPH:
                    scores(i - 1)
                    latent_input()
                if f == 0:
                    w_wait(pe, ("wq again", 0) if again and j == 0 else ("wq", j))
                if i >= 2:
                    pe.wait_ge(S("q_ok"), i - 1)
                w = ring[slot_of["wq again", 0] if again and j == 0 else slot_of["wq", j]]
                for k in range(KD):
                    if again:
                        m = pe.matmul(ps[:, i % 2, :], w[:, k, P * f:P * f + P], hT[:, k, LC:T], start=(k == 0), stop=(k == KD - 1))
                    else:
                        m = pe.matmul(ps[:, 2 + i % 2, 0:LC], w[:, k, P * f:P * f + P], hT[:, k, 0:LC], start=(k == 0), stop=(k == KD - 1))
                m.then_inc(S("q_mm"), 1)
                if i >= 1 and i != 2 * EXPH:
                    scores(i - 1)
            scores(4 * EXPH - 1)

        @block.scalar
        def _(act):
            own = Own(act, S("act_ch"))
            A = act.activation
            act.wait_ge(S("cols_ok"), 1)
            own.do(A(csil[:, :, :].rearrange("p a b -> p (a b)"), cols[:, 48:64], ACT.Sigmoid), S("sig_c"))

            def norm_sq(first):
                for t in range(NT):
                    own.do(A(xn[:, t, :], x[:, t, :], ACT.Square, accum_out=stat[:, t:t + 1]), S("sq_ok"))
                act.wait_ge(S("ms_ok"), first + 1)
                own.do(A(stat[:, 16:16 + NT], stat[:, 8:8 + NT], ACT.Sqrt), S("rt_ok"))

            act.wait_ge(S("ld_x"), 32)
            norm_sq(0)

            def norm_mod(first, shift):
                act.wait_ge(S("amp_ok"), first + 1)
                for k in range(KD):
                    act.wait_ge(S("xT_mm"), first * KD + k + 1)
                    A(hT[:, k, LC:T], ps[:, k % 3, :], ACT.Identity, bias=mod[:, shift + k, 1:2], scale=amp[:, k, 1:2])
                    own.do(A(hT[:, k, 0:LC], ps[:, 3 + k % 3, 0:P], ACT.Identity, bias=mod[:, shift + k, 0:1],
                             scale=amp[:, k, 0:1]), S("hT_ok"))

            norm_mod(0, 0)

            def rows_out(c):
                for t in range(NT):
                    i = NT * c + t
                    act.wait_ge(S("uT_mm"), i + 1)
                    dst = rkv[:, t, c, :] if c < 3 else hv[:, t, c - 3, :]
                    own.do(A(dst, ps[:, 4 + i % 2, :], ACT.Copy), S("u_ok"))

            for n in range(NIN):
                c, f = divmod(n, 4)
                act.wait_ge(S("in_mm"), n + 1)
                if c >= 2 and f == 0:
                    act.wait_ge(S("uT_mm"), NT * (c - 1))
                w1 = colsB[:, NIN + n:NIN + n + 1]
                A(yT[:, c % 2, f, LC:T], ps[:, n % 2, :], ACT.Copy, scale=w1)
                own.do(A(yT[:, c % 2, f, 0:LC], ps[:, 2 + n % 2, 0:LC], ACT.Copy, scale=w1), S("conv_mid"))
                if f == 1 and c >= 1:
                    rows_out(c - 1)
            rows_out(5)
            for i, (bl, bc, dst, fn) in enumerate(((0, 2, tanhT, ACT.Tanh), (1, 3, aloT, ACT.Copy), (4, 5, gateT, ACT.Sigmoid))):
                act.wait_ge(S("lora_mm"), i + 1)
                A(dst[:, LC:T], ps[:, bl, :], fn)
                own.do(A(dst[:, 0:LC], ps[:, bc, 0:LC], fn), S("lora_ok"))
            act.wait_ge(S("kk_sq"), 1)
            own.do(A(bon[:, :, :].rearrange("p a b -> p (a b)"), bon[:, :, :].rearrange("p a b -> p (a b)"), ACT.Sqrt), S("kk_rt"))
            def prepare(n):
                if n >= len(UNITS):
                    while True:
                        yield
                for i, v in enumerate((wsg, av)):
                    act.wait_ge(S("r_pre"), 2 * n + 1 + i)
                    own.do(A(v, v, ACT.Sigmoid), S("r_sig"))
                    yield
                act.wait_ge(S("r_cum"), 2 * n + 1)
                if n:
                    act.wait_ge(S("r_x0"), 2 * n)
                for dst, b, sign in ((pi_, 0, 1.0), (pinv, 0, -1.0), (pex, 7, 1.0)):
                    own.do(A(dst, ps[:, b, :], ACT.Exp, scale=sign), S("r_exp"))
                    yield
                act.wait_ge(S("r_cum"), 2 * n + 2)
                own.do(A(pc2[n % 2][:, :, :].rearrange("p a b -> p (a b)"), ps[:, 0, 0:2 * PAIRS], ACT.Exp), S("r_exp"))
                yield
                for p in range(PAIRS):
                    act.wait_ge(S("r_tr"), 4 * n + p + 1)
                    own.do(A(tt2[n % 2][:, p, :, :].rearrange("p a b -> p (a b)"), ps[:, 7 * (p % 2), :], ACT.Copy), S("r_tt"))
                    yield
                while True:
                    yield

            def start_x(n):
                act.wait_ge(S("r_ops"), n + 1)
                if n >= 1:
                    act.wait_ge(S("r_yl"), n)
                own.do(A(xs[:, :, 0, :, :].rearrange("p u i j -> p u (i j)"), pex.rearrange("p (u x) -> p u x", x=P), ACT.Copy), S("r_x0"))

            first = prepare(0)
            for _ in range(10):
                next(first)
            start_x(0)
            for n, (t, d) in enumerate(UNITS):
                act.wait_ge(S("r_s2"), n + 1)
                own.do(A(xs[:, :, 1, :, :].rearrange("p u i j -> p u (i j)"), ps[:, 0, :].rearrange("p (u x) -> p u x", x=P), ACT.Copy), S("r_x0"))
                ahead = prepare(n + 1)
                for l in range(LEVELS):
                    for g in range(2):
                        if l < LEVELS - 1:
                            act.wait_ge(S("r_lv"), 12 * n + 2 * l + g + 1)
                            own.do(A(nn[:, 4 * g:4 * g + 4, :, :].rearrange("p h i t -> p i h t"),
                                     ps[:, 2 + 3 * g:4 + 3 * g, :].rearrange("p i (h t) -> p i h t", t=P), ACT.Copy), S("r_lvn"))
                        for _ in range(PREP_ACT.get(2 * l + g, 0)):
                            next(ahead)
                act.wait_ge(S("r_hm"), n + 1)
                if n >= 1:
                    act.wait_ge(S("r_st"), 2 * n)
                for i in range(2):
                    q = slice(64 * i, 64 * i + 64)
                    m = A(hc[q, :, :, 64 * i:64 * i + 64], ps[q, 2:4, :].rearrange("p c (a b) -> p c a b", b=P)[:, :, :, 64 * i:64 * i + 64], ACT.Copy)
                own.do(m, S("r_hc"))
                if n + 1 < len(UNITS):
                    start_x(n + 1)
            act.wait_ge(S("gn_var"), 1)
            own.do(A(KK[:, 0, 0:40], KK[:, 0, 0:40], ACT.Sqrt), S("gn_rt"))

            def mix_out(which):
                for k in range(4):
                    act.wait_ge(S("yb_T" if which else "ya_T"), k + 1)
                    A(hT[:, 4 * which + k, LC:T], ps[:, 2 + 2 * (k % 2), :], ACT.Copy)
                    own.do(A(hT[:, 4 * which + k, 0:LC], ps[:, 3 + 2 * (k % 2), 0:LC], ACT.Copy), S("mix_ok"))

            mix_out(0)
            for i in range(2):
                act.wait_ge(S("arg_ok"), i + 1)
                own.do(A(hid[0:HD, :], harg[0:HD, 2, :], ACT.Sin), S("sin_ok"))
            ng = 0
            for tiles, _, _ in SEQS(fctx, ictx, ftab, itab):
                for o in range(2):
                    for k in range(len(tiles)):
                        act.wait_ge(S("hg_mm"), ng + 1)
                        b = 4 + 2 * (ng % 2)
                        if len(tiles) > 1 and k == 0 and o == 0:
                            act.wait_ge(S("hy_ok"), 2)
                        own.do(A(gf[:, o, :, k, :], ps[:, b:b + 2, :], ACT.Copy), S("hg_ok"))
                        ng += 1
            act.wait_ge(S("hz_ok"), 2 * NT)
            act.wait_ge(S("hy_ok"), 2 * NT)
            for t in range(NT):
                own.do(A(yf[:, 0, t % 4, :] if t < 4 else yf[:, 1, 0, :], hv[:, t, 0, :], ACT.Square, accum_out=stat[:, 32 + t:33 + t]), S("zsq_ok"))
            act.wait_ge(S("zms_ok"), 1)
            own.do(A(stat[:, 48:48 + NT], stat[:, 40:40 + NT], ACT.Sqrt), S("zrt_ok"))
            mix_out(1)
            act.wait_ge(S("gate_mm"), 1)
            own.do(A(gbc[:, :, :].rearrange("p c n -> p (c n)"), ps[:, 0:4, :].rearrange("p a b -> p (a b)"), ACT.Copy), S("gate_ok"))
            def norm2_sq(tiles, part):
                act.wait_ge(S("x2_ok"), 2 * tiles.stop)
                for t in tiles:
                    own.do(A(xn2[:, t, :], x[:, t, :], ACT.Square, accum_out=stat[:, t:t + 1]), S("n2_sq"))
                act.wait_ge(S("n2_ms"), part + 1)
                own.do(A(stat[:, 16 + tiles.start:16 + tiles.stop], stat[:, 8 + tiles.start:8 + tiles.stop], ACT.Sqrt), S("n2_rt"))

            norm2_sq(range(0, 1), 0)
            act.wait_ge(S("amp_ok"), 2)
            for k in range(KD):
                act.wait_ge(S("n2_T"), 1 + k // 4)
                own.do(A(hT[:, k, 0:LC], ps[:, 6 + k // 4, P * (k % 4):P * (k % 4) + P], ACT.Identity, bias=mod[:, 24 + k, 0:1],
                         scale=amp[:, k, 0:1]), S("h2T_ok"))
            norm2_sq(range(1, NT), 1)
            for g in range(4):
                act.wait_ge(S("key_mm"), g + 1)
                own.do(A(keyT[:, 4 * g:4 * g + 4, :].rearrange("p a b -> p (a b)"), ps[:, g, :], ACT.Copy), S("key_ok"))

            def latent_input():
                for k in range(KD):
                    act.wait_ge(S("n2_T"), 2 + k + 1)
                    own.do(A(hT[:, k, LC:T], ps[:, k % 2, :], ACT.Identity, bias=mod[:, 24 + k, 1:2], scale=amp[:, k, 1:2]), S("h2T_ok"))
                for i in range(2 * NT):
                    act.wait_ge(S("h2_mm"), i + 1)
                    own.do(A(h2[:, i // 2, 512 * (i % 2):512 * (i % 2) + 512], ps[:, 4 + i % 2, :], ACT.Copy), S("h2_ok"))
                act.wait_ge(S("gate_mm"), 2)
                own.do(A(g2bc[:, :, :].rearrange("p c n -> p (c n)"), ps[:, 0:4, :].rearrange("p a b -> p (a b)"), ACT.Copy), S("gate_ok"))

            tsf = ts[:, :, :].rearrange("p a b -> p (a b)")

            def sc_out(i):
                n = QORDER[i]
                act.wait_ge(S("sc_mm"), i + 1)
                if i < 2 * EXPH:
                    own.do(A(sco[:, 0, n, :], ps[:, 7, 0:NKEY], ACT.Copy), S("sc_ok"))
                else:
                    own.do(A(sco[:, 1:NT, n, :], ps[:, 6, :].rearrange("p (t k) -> p t k", k=NKEY), ACT.Copy), S("sc_ok"))

            for i in range(4 * EXPH):
                if i == 2 * EXPH:
                    sc_out(i - 1)
                    latent_input()
                act.wait_ge(S("q_mm"), i + 1)
                if i >= 2:
                    act.wait_ge(S("sc_mm"), i - 1)
                if i < 2 * EXPH:
                    own.do(A(qbuf[:, i % 2, 0:LC], ps[:, 2 + i % 2, 0:LC], ACT.Copy), S("q_ok"))
                else:
                    own.do(A(qbuf[:, i % 2, LC:T], ps[:, i % 2, :], ACT.Copy), S("q_ok"))
                if i >= 1 and i != 2 * EXPH:
                    sc_out(i - 1)
                if i == 2 * EXPH + 3:
                    act.wait_ge(S("top_sub"), 1)
                    A(tsf, tsf, ACT.Exp).then_inc(S("top_exp"), 1)
            sc_out(4 * EXPH - 1)
            act.wait_ge(S("g_used"), RING + SLOTS)
            A(dots, dots, ACT.Gelu).then_inc(S("gelu_ok"), 1)
            act.wait_ge(S("top_sub"), 2)
            A(tsf, tsf, ACT.Exp).then_inc(S("top_exp"), 1)
            with act.Fori(1, NT - 1) as i:
                act.wait_ge(S("top_sub"), i + 2)
                A(tsf, tsf, ACT.Exp).then_inc(S("top_exp"), 1)
                act.wait_ge(S("g_used"), i * (2 * SLOTS) + RING + SLOTS)
                A(dots, dots, ACT.Gelu).then_inc(S("gelu_ok"), 1)
            act.wait_ge(S("g_used"), (NT - 1) * 2 * SLOTS + RING + SLOTS)
            A(dots, dots, ACT.Gelu).then_inc(S("gelu_ok"), 1)
            act.wait_ge(S("x3_ok"), NT)
            for t in range(NT):
                A(sqj[:, t, :], x[:, t, :], ACT.Square, accum_out=stat[:, t:t + 1]).then_inc(S("fsq_ok"), 1)
            act.wait_ge(S("fms_ok"), 1)
            A(stat[:, 16:16 + NT], stat[:, 8:8 + NT], ACT.Sqrt).then_inc(S("frt_ok"), 1)

        @block.vector
        def _(dve):
            own = Own(dve, S("dve_ch"))
            V = dve
            dve.wait_ge(S("rows_T"), 1)
            V.tensor_copy(cols, ps[:, 0, 0:P])
            own.do(V.tensor_copy(colsB, ps[:, 0, P:2 * P]), S("cols_ok"))
            dve.wait_ge(S("sig_c"), 1)
            own.settle()
            cs = csil.rearrange("p a b -> p (a b)")
            own.do(V.tensor_tensor(cs, cs, cols[:, 48:64], ALU.mult), S("csil_ok"))

            def norm_rows(first):
                dve.wait_ge(S("sq_ok"), NT * (first + 1))
                own.do(V.tensor_scalar(stat[:, 8:8 + NT], stat[:, 0:NT], 1.0 / D, EPS, ALU.mult, ALU.add), S("ms_ok"))
                dve.wait_ge(S("rt_ok"), first + 1)
                own.do(V.reciprocal(stat[:, 24:24 + NT], stat[:, 16:16 + NT]))
                own.settle()
                for t in range(NT):
                    i = V.tensor_scalar(xn[:, t, :], x[:, t, :], stat[:, 24 + t:25 + t], None, ALU.mult)
                own.do(i, S("xn_ok"))

            norm_rows(0)

            def mod_out(j):
                dve.wait_ge(S("ada_mm"), j + 1)
                o = mod[:, 4 * j:4 * j + 4, :]
                own.do(V.tensor_tensor(o, ps[:, 6 + j % 2, 0:8].rearrange("p (a b) -> p a b", b=2),
                                       cols[:, 4 * j:4 * j + 4].unsqueeze(2).to_broadcast([P, 4, 2]), ALU.add), S("mod_ok"))

            def amplitude(scale, gain):
                own.settle()
                own.do(V.scalar_tensor_tensor(amp, mod[:, scale:scale + KD, :], 1.0,
                                              cols[:, gain:gain + KD].unsqueeze(2).to_broadcast([P, KD, 2]),
                                              ALU.add, ALU.mult), S("amp_ok"))

            for j in range(4):
                mod_out(j)
            amplitude(8, 64)
            for n in range(NIN):
                c, f = divmod(n, 4)
                dve.wait_ge(S("conv_mid"), n + 1)
                for j, (shift_o, shift_i) in enumerate(((1, 0), (0, 1))):
                    w = colsB[:, (0, 2)[j] * NIN + n:(0, 2)[j] * NIN + n + 1]
                    lat = yT[:, c % 2, f, LC:T].rearrange("p (r g) -> p r g", g=GRID)
                    lin = ps[:, n % 2, :].rearrange("p (r g) -> p r g", g=GRID)
                    o = lat[:, :, shift_o:shift_o + GRID - 1]
                    if j:
                        own.settle()
                    own.do(V.scalar_tensor_tensor(o, lin[:, :, shift_i:shift_i + GRID - 1], w, o, ALU.mult, ALU.add))
                    o = yT[:, c % 2, f, shift_o:shift_o + LC - 1]
                    own.do(V.scalar_tensor_tensor(o, ps[:, 2 + n % 2, shift_i:shift_i + LC - 1], w, o, ALU.mult, ALU.add),
                           S("conv_ok") if j else None)
                if f == 3 and c < 4:
                    mod_out(4 + 2 * c)
                    mod_out(5 + 2 * c)
            bonf = bon[:, :, :].rearrange("p a b -> p (a b)")
            dve.wait_ge(S("u_ok"), 6 * NT)
            dve.wait_ge(S("lora_ok"), 3)
            dve.wait_ge(S("ld_rw"), 16 * RWLOADS)
            for t in range(NT):
                own.do(V.tensor_tensor(KK[:, t, :], rkv[:, t, 1, :], vec["k_k"], ALU.mult))
            own.settle()
            sq = Y[:, :, :].rearrange("p t (h j) -> p t h j", j=HD)
            own.do(V.tensor_tensor(Y, KK, KK, ALU.mult))
            own.settle()
            own.do(V.tensor_reduce(bon, sq, AX.X, ALU.add))
            own.settle()
            own.do(V.tensor_scalar(bonf, bonf, 1e-24, None, ALU.max), S("kk_sq"))
            dve.wait_ge(S("kk_rt"), 1)
            own.do(V.reciprocal(bonf, bonf))
            own.settle()
            for t in range(NT):
                k = KK[:, t, :].rearrange("p (h j) -> p h j", j=HD)
                own.do(V.tensor_tensor(k, k, bon[:, t, :].unsqueeze(2).to_broadcast([P, HEADS, HD]), ALU.mult))
            own.settle()
            V.memset(bonf, 0.0)
            V.memset(Y, 0.0)
            V.memset(gblk, 0.0)
            V.memset(st2[0], 0.0)
            own.do(V.memset(hc, 0.0), S("rw_zero"))
            own.settle()
            dve.wait_ge(S("st_mm"), 1)
            own.do(V.tensor_copy(st2[1][:, :, :, :].rearrange("p e a b -> p e (a b)"), ps[:, 2:4, :]), S("st_in"))

            def prepare(n):
                if n >= len(UNITS):
                    while True:
                        yield
                t, d = UNITS[n]
                R, K, kd, bt = rkv[:, t, 0, :], rkv[:, t, 1, :], kd2[n % 2], bt2[n % 2]
                dve.wait_ge(S("r_lora"), n + 1)
                own.do(V.tensor_tensor(wsg, ps[:, 0, :], vec["w0"][:, d, :], ALU.add), S("r_pre"))
                yield
                own.do(V.tensor_tensor(av, ps[:, 7, :], vec["a0"][:, d, :], ALU.add), S("r_pre"))
                yield
                dve.wait_ge(S("r_sig"), 2 * n + 2)
                own.do(V.scalar_tensor_tensor(kd, av, -1.0, vec["k_a"], ALU.add, ALU.mult))
                yield
                own.settle()
                own.do(V.scalar_tensor_tensor(kd, kd, 1.0, K, ALU.add, ALU.mult))
                yield
                own.settle()
                own.do(V.tensor_tensor(bt, kd, R, ALU.mult))
                own.do(V.tensor_tensor(av, av, KK[:, t, :], ALU.mult))
                yield
                own.settle()
                own.do(V.tensor_tensor(bt, bt, vec["r_k"][:, d, :], ALU.mult))
                yield
                own.settle()
                own.do(V.tensor_reduce(hn[:, 0:HEADS], bt.rearrange("p (h j) -> p h j", j=HD), AX.X, ALU.add))
                own.settle()
                own.do(V.tensor_tensor(bon[:, t, :], bon[:, t, :], hn[:, 0:HEADS], ALU.add))
                yield
                dve.wait_ge(S("r_exp"), 4 * n + 3)
                V.scalar_tensor_tensor(bt, av, -1.0, pinv, ALU.mult, ALU.mult)
                yield
                V.tensor_tensor(pex, pex, KK[:, t, :], ALU.mult)
                V.tensor_tensor(pi_, pi_, R, ALU.mult)
                yield
                own.do(V.tensor_tensor(kd, kd, pinv, ALU.mult), S("r_ops"))
                while True:
                    yield

            def mask(n, p):
                d = UNITS[n][1]
                b = 4 * (p % 2)
                dve.wait_ge(S("r_s1"), 4 * n + p + 1)
                V.tensor_tensor(lm[:, 2 * p:2 * p + 2, :, :].rearrange("p h (m e) t -> p (h m) (e t)", e=2),
                                ps[:, b:b + 2, :].rearrange("p h (m x) -> p (h m) x", m=2),
                                lmask[:, d, 0:2, :].rearrange("p a b -> p (a b)").unsqueeze(1).to_broadcast([P, 4, 2 * P]), ALU.mult)
                own.do(V.tensor_tensor(nn[:, 2 * p:2 * p + 2, 0, :], ps[:, b + 2:b + 4, 0:P],
                                       lmask[:, d, 2:3, :].to_broadcast([P, 2, P]), ALU.mult), S("r_mask"))

            first = prepare(0)
            for _ in range(10):
                next(first)
            mask(0, 0)
            mask(0, 1)
            for n, (t, d) in enumerate(UNITS):
                tt, pc, st = tt2[n % 2], pc2[n % 2], st2[min(t, 1)]
                mask(n, 2)
                mask(n, 3)
                ahead = prepare(n + 1)
                for l in range(LEVELS):
                    for g in range(2):
                        dve.wait_ge(S("r_lv"), 12 * n + 2 * l + g + 1)
                        if l == 0 and g == 0:
                            dve.wait_ge(S("r_x0"), 2 * n + 2)
                        xg = xs[:, 2 * g:2 * g + 2, :, :, :].rearrange("p u k i j -> p (u k i j)")
                        own.do(V.tensor_tensor(xg, ps[:, 1 + 3 * g, :], xg, ALU.add), S("r_lvx"))
                        for _ in range(PREP_DVE.get(2 * l + g, 0)):
                            next(ahead)
                dve.wait_ge(S("r_g"), n + 1)
                for i in range(2):
                    q = slice(64 * i, 64 * i + 64)
                    for c in range(2):
                        V.tensor_tensor(gblk[q, c, :, 64 * i:64 * i + 64],
                                        ps[q, 7 * c, :].rearrange("p (a b) -> p a b", b=P)[:, :, 64 * i:64 * i + 64],
                                        i64[q, :].unsqueeze(1).to_broadcast([64, PAIRS, HD]), ALU.add)
                dve.wait_ge(S("r_q"), n + 1)
                own.do(V.tensor_tensor(qT, ps[:, 1, :].rearrange("p (a b) -> p a b", b=P), tt[:, :, 1, :], ALU.add), S("r_gq"))
                dve.wait_ge(S("r_yl"), n + 1)
                own.settle()
                own.do(V.tensor_tensor(Y[:, t, :], ps[:, 5, :], Y[:, t, :], ALU.add))
                dve.wait_ge(S("r_hc"), n + 1)
                for k, c in enumerate((0, 1) if d == 0 else (1, 0)):
                    dve.wait_ge(S("r_step"), 2 * n + k + 1)
                    own.do(V.tensor_tensor(st[:, d, :, :], ps[:, 4, :].rearrange("p (a b) -> p a b", b=P), hc[:, c, :, :], ALU.add))
                    own.settle()
                    own.do(V.tensor_tensor(st[:, d, :, :], st[:, d, :, :], pc[:, :, c:c + 1].to_broadcast([P, PAIRS, P]), ALU.mult), S("r_st"))
                    if k == 0 and n + 1 < len(UNITS):
                        mask(n + 1, 0)
                own.do(V.tensor_tensor(Y[:, t, :], ps[:, 6, :], Y[:, t, :], ALU.add), S("unit_ok"))
                if n == 1:
                    dve.wait_ge(S("sn_mm"), 1)
                    own.do(V.tensor_copy(sn[:, :, :, :].rearrange("p e a b -> p e (a b)"), ps[:, 4:6, :]), S("sn_ok"))
                if n + 1 < len(UNITS):
                    mask(n + 1, 1)
            own.settle()
            Yh = Y[:, :, :].rearrange("p t (h j) -> p (t h) j", j=HD)
            Kh = KK[:, :, :].rearrange("p t (h j) -> p (t h) j", j=HD)
            TH = NT * HEADS
            mu, var = vec["k_k"][:, 0:TH], KK[:, 0, 0:TH]
            bc = lambda v: v.unsqueeze(2).to_broadcast([P, TH, HD])
            chain = lambda i: (own.do(i), own.settle())
            chain(V.tensor_reduce(mu, Yh, AX.X, ALU.add))
            chain(V.tensor_scalar(mu, mu, 1.0 / HD, None, ALU.mult))
            chain(V.tensor_tensor(Yh, Yh, bc(mu), ALU.subtract))
            chain(V.tensor_tensor(Kh, Yh, Yh, ALU.mult))
            chain(V.tensor_reduce(mu, Kh, AX.X, ALU.add))
            own.do(V.tensor_scalar(var, mu, 1.0 / HD, GN_EPS, ALU.mult, ALU.add), S("gn_var"))
            dve.wait_ge(S("gn_rt"), 1)
            chain(V.reciprocal(mu, var))
            chain(V.tensor_tensor(Yh, Yh, bc(mu), ALU.mult))
            over = lambda v: v.unsqueeze(1).to_broadcast([P, NT, DR])
            chain(V.tensor_tensor(Y, Y, over(vec["ln_w"]), ALU.mult))
            chain(V.tensor_tensor(Y, Y, over(vec["ln_b"]), ALU.add))
            for t in range(NT):
                own.do(V.tensor_tensor(KK[:, t, :].rearrange("p (h j) -> p h j", j=HD), rkv[:, t, 2, :].rearrange("p (h j) -> p h j", j=HD),
                                       bon[:, t, :].unsqueeze(2).to_broadcast([P, HEADS, HD]), ALU.mult))
            own.settle()
            chain(V.tensor_tensor(Y, Y, KK, ALU.add))
            for t in range(NT):
                dve.wait_ge(S("g_mm"), t + 1)
                own.do(V.tensor_tensor(Y[:, t, :], Y[:, t, :], ps[:, t % 2, :], ALU.mult), S("gm_ok"))
            for i in range(2):
                dve.wait_ge(S("hid_mm"), i + 1)
                q = slice(0, HD)
                b, f = cols[q, 80 + i:81 + i], cols[q, 82 + i:83 + i]
                V.tensor_scalar(harg[q, 0, 0:LL], ps[q, 0, :], b, f, ALU.add, ALU.mult)
                own.do(V.tensor_scalar(harg[q, 0, LL:T], ps[q, 1, 0:LC], b, f, ALU.add, ALU.mult))
                own.settle()
                chain(V.tensor_scalar(harg[q, 1, :], harg[q, 0, :], 1.0 / (2 * math.pi), ROUND, ALU.mult, ALU.add))
                chain(V.tensor_scalar(harg[q, 1, :], harg[q, 1, :], ROUND, None, ALU.subtract))
                chain(V.scalar_tensor_tensor(harg[q, 2, :], harg[q, 1, :], -TWO_PI[0], harg[q, 0, :], ALU.mult, ALU.add))
                chain(V.scalar_tensor_tensor(harg[q, 2, :], harg[q, 1, :], -TWO_PI[1], harg[q, 2, :], ALU.mult, ALU.add))
                own.do(V.tensor_scalar(harg[q, 2, :], harg[q, 2, :], PI_IN, -PI_IN, ALU.min, ALU.max), S("arg_ok"))
            nf = ng = nu = ni = 0
            for tiles, _, _ in SEQS(fctx, ictx, ftab, itab):
                nk = len(tiles)
                for o in range(2):
                    if ng:
                        dve.wait_ge(S("hg_mm"), ng)
                    if nk > 1 and o == 0:
                        dve.wait_ge(S("hi_mm"), 2)
                    if nf == 0:
                        dve.wait_ge(S("sin_ok"), 2)
                    for j, t in enumerate(tiles):
                        b = 2 * (nf % 2)
                        dve.wait_ge(S("hf_mm"), nf + 1)
                        if nf:
                            own.settle()
                        V.tensor_tensor(htmp[:, 0, :], ps[:, b, :], win[:, t, :], ALU.mult)
                        chain(V.tensor_tensor(htmp[:, 1, :], ps[:, b + 1, :], win[:, t, :], ALU.mult))
                        own.do(V.tensor_tensor(yf[:, 0, j, :], htmp[:, 0, :], htmp[:, 1, :], ALU.add))
                        if j == 0:
                            own.settle()
                            own.do(V.tensor_tensor(yf[0:1, 0, 0, :], yf[0:1, 0, 0, :], hbias[0:1, DR * o:DR * o + DR], ALU.add))
                        own.do(V.tensor_tensor(yf[:, 1, j, :], htmp[:, 0, :], htmp[:, 1, :], ALU.subtract), S("hf_ok"))
                        nf += 1
                    ng += nk
                for o in range(2):
                    dve.wait_ge(S("hg_mm"), ng)
                    dve.wait_ge(S("hg_ok"), ng)
                    if ni:
                        dve.wait_ge(S("hi_mm"), ni)
                    for k in range(nk):
                        b = 2 * (nu % 2)
                        dve.wait_ge(S("hu_mm"), nu + 1)
                        own.settle()
                        gc, gs = gf[:, o, 0, k, :], gf[:, o, 1, k, :]
                        V.tensor_tensor(yf[:, 0, k, :], ps[:, b, :], gc, ALU.mult)
                        V.tensor_tensor(htmp[:, 0, :], ps[:, b + 1, :], gs, ALU.mult)
                        V.tensor_tensor(yf[:, 1, k, :], ps[:, b + 1, :], gc, ALU.mult)
                        chain(V.tensor_tensor(htmp[:, 1, :], ps[:, b, :], gs, ALU.mult))
                        V.tensor_tensor(yf[:, 0, k, :], yf[:, 0, k, :], htmp[:, 0, :], ALU.subtract)
                        own.do(V.tensor_tensor(yf[:, 1, k, :], yf[:, 1, k, :], htmp[:, 1, :], ALU.add), S("hy_ok"))
                        nu += 1
                    for t in tiles:
                        dve.wait_ge(S("hi_mm"), ni + 1)
                        own.do(V.tensor_tensor(hv[:, t, 0, :], ps[:, 4 + ni % 2, :], hv[:, t, 1 + o, :], ALU.mult), S("hz_ok"))
                        ni += 1
            dve.wait_ge(S("zsq_ok"), NT)
            own.do(V.tensor_scalar(stat[:, 40:40 + NT], stat[:, 32:32 + NT], 1.0 / DR, EPS, ALU.mult, ALU.add), S("zms_ok"))
            dve.wait_ge(S("zrt_ok"), 1)
            chain(V.reciprocal(stat[:, 56:56 + NT], stat[:, 48:48 + NT]))
            dve.wait_ge(S("ld_hn"), 16)
            for t in range(NT):
                own.do(V.scalar_tensor_tensor(hv[:, t, 0, :], hv[:, t, 0, :], stat[:, 56 + t:57 + t], hnorm, ALU.mult, ALU.mult), S("yb_ok"))
            dve.wait_ge(S("gate_ok"), 1)
            dve.wait_ge(S("ld_x"), 64)
            def norm2_rows(tiles, part):
                a8, a16, a24 = (stat[:, c + tiles.start:c + tiles.stop] for c in (8, 16, 24))
                dve.wait_ge(S("n2_sq"), tiles.stop)
                own.do(V.tensor_scalar(a8, stat[:, tiles.start:tiles.stop], 1.0 / D, EPS, ALU.mult, ALU.add), S("n2_ms"))
                dve.wait_ge(S("n2_rt"), part + 1)
                own.do(V.reciprocal(a24, a16))
                own.settle()
                for t in tiles:
                    m = V.tensor_scalar(xn2[:, t, :], x[:, t, :], stat[:, 24 + t:25 + t], None, ALU.mult)
                own.do(m, S("n2_xn"))

            amplitude(32, 72)
            for i, (t, j) in enumerate(OUT_ORDER):
                dve.wait_ge(S("out_mm"), i + 1)
                q = slice(512 * j, 512 * j + 512)
                if i:
                    own.settle()
                own.do(V.tensor_tensor(omul[:, i % 2, :], ps[:, 4 + i % 2, :], gbc[:, min(t, 1), q], ALU.mult))
                own.settle()
                own.do(V.tensor_tensor(x[:, t, q], x[:, t, q], omul[:, i % 2, :], ALU.add), S("x2_ok"))
                if i == 1:
                    norm2_rows(range(0, 1), 0)
            norm2_rows(range(1, NT), 1)
            dve.wait_ge(S("ld_io"), 16)
            f3 = lambda v: v[:, :, :].rearrange("p a b -> p (a b)")

            def top_of(vals, n, width_v, width_i):
                for half in range(2):
                    o = slice(8 * half, 8 * half + 8)
                    for r in range(n):
                        m = V.max(width_v[:, r, o], vals[:, r, :])
                        if r < n - 1:
                            yield
                    rown.do(m)
                    yield
                    rown.settle()
                    for r in range(n):
                        m = V.max_index(width_i[:, r, o], width_v[:, r, o], vals[:, r, :])
                        if r < n - 1:
                            yield
                    rown.do(m)
                    yield
                    rown.settle()
                    if not half:
                        for r in range(n):
                            m = V.match_replace(vals[:, r, :], width_v[:, r, o], vals[:, r, :], -3.0e38)
                            if r < n - 1:
                                yield
                        rown.do(m)
                        yield
                        rown.settle()

            def route(t, n):
                rown.do(V.tensor_copy(f3(scur), sco[:, t:t + 1, :, :].rearrange("p a b c -> p (a b c)") if isinstance(t, int)
                                    else sco[:, bass.ds(t, 1), :, :].rearrange("p a b c -> p (a b c)")))
                yield
                rown.settle()
                yield from top_of(scur, 2 * EXPH, sv, si)
                V.tensor_copy(f3(sif), f3(si))
                sv4 = sv[:, :, :].rearrange("p (h e) k -> p h e k", e=2)
                c4 = cand[:, :, :].rearrange("p h (a b) -> p h a b", b=TOPK)
                rown.do(V.tensor_tensor(c4, sv4[:, :, 0, :].unsqueeze(3).to_broadcast([P, EXPH, TOPK, TOPK]),
                                      sv4[:, :, 1, :].unsqueeze(2).to_broadcast([P, EXPH, TOPK, TOPK]), ALU.add))
                yield
                rown.settle()
                yield from top_of(cand, EXPH, ts, tp)
                V.tensor_scalar(f3(ti), f3(tp), 4, None, ALU.logical_shift_right)
                rown.do(V.tensor_scalar(f3(tp), f3(tp), TOPK - 1, None, ALU.bitwise_and))
                yield
                rown.settle()
                sf4 = sif[:, :, :].rearrange("p (h e) k -> p h e k", e=2)
                for e, pos in ((0, ti), (1, tp)):
                    rown.do(V.tensor_copy(f3(tj), f3(pos)))
                    yield
                    rown.settle()
                    rown.do(V.tensor_tensor(onehot, tj[:, :, :].unsqueeze(3).to_broadcast([P, EXPH, TOPK, TOPK]),
                                          iota16.unsqueeze(1).unsqueeze(1).to_broadcast([P, EXPH, TOPK, TOPK]), ALU.is_equal))
                    yield
                    rown.settle()
                    rown.do(V.tensor_tensor(onehot, onehot, sf4[:, :, e, :].unsqueeze(2).to_broadcast([P, EXPH, TOPK, TOPK]), ALU.mult))
                    yield
                    rown.settle()
                    rown.do(V.tensor_reduce(eid[e], onehot, AX.X, ALU.add))
                    yield
                    rown.settle()
                rown.do(V.scalar_tensor_tensor(f3(eid[2]), f3(eid[0]), float(NKEY), f3(eid[1]), ALU.mult, ALU.add))
                yield
                rown.settle()
                col = (lambda v: v[:, t:t + 1, :].rearrange("p a b -> p (a b)")) if isinstance(t, int) else (lambda v: v[:, bass.ds(t, 1), :].rearrange("p a b -> p (a b)"))
                V.tensor_copy(col(eall), f3(eid[2])).then_inc(S("eid_ok"), 1)
                rown.do(V.tensor_copy(tsum[:, 0:EXPH], ts[:, :, 0]))
                yield
                rown.settle()
                V.tensor_tensor(ts, ts, tsum[:, 0:EXPH].unsqueeze(2).to_broadcast([P, EXPH, TOPK]), ALU.subtract).then_inc(S("top_sub"), 1)
                yield
                dve.wait_ge(S("top_exp"), n)
                rown.do(V.tensor_reduce(tsum[:, 0:EXPH], ts, AX.X, ALU.add))
                yield
                rown.settle()
                rown.do(V.reciprocal(tsum[:, EXPH:2 * EXPH], tsum[:, 0:EXPH]))
                yield
                rown.settle()
                rown.do(V.tensor_tensor(col(wall).rearrange("p (h k) -> p h k", k=TOPK), ts, tsum[:, EXPH:2 * EXPH].unsqueeze(2).to_broadcast([P, EXPH, TOPK]), ALU.mult))
                yield
                rown.settle()

            own.settle()
            own = rown = Own(dve, S("route_ch"))
            dve.sem_inc(S("g_used"), RING)
            dve.wait_ge(S("sc_ok"), 2 * EXPH)
            per_yield = sum(1 for _ in route(0, 1))
            per_route = rown.count[id(S("route_ch"))]

            def row(t, e, m):
                dve.wait_ge(row_here[m % RING], (t * (2 * SLOTS // RING) + (e - 1) * (SLOTS // RING) + m // RING + 1) * 16)
                dve.wait_ge(S("g_used"), t * (2 * SLOTS) + e * SLOTS + m + RING - 1)

            def dot(m, slot, h):
                V.scalar_tensor_tensor(junk[:, m % 2, :], slot, 1.0, h, ALU.mult, ALU.mult,
                                       accum_out=dots[:, m:m + 1]).then_inc(S("g_used"), 1)

            def spread_over(parts, m, rows):
                for _ in range((m + 1) * per_yield // rows - m * per_yield // rows):
                    next(parts, None)

            def weigh_and_sum(t, parts=None):
                dve.wait_ge(S("gelu_ok"), t + 1)
                V.tensor_tensor(coef, dots, wall[:, bass.ds(t, 1), :].rearrange("p a b -> p (a b)"), ALU.mult).then_inc(S("ex_ch"), 1)
                dve.wait_ge(S("ex_ch"), t * 4 + 3)
                for m in range(SLOTS):
                    row(t, 1, m)
                    V.scalar_tensor_tensor(acc[:, m % 2, :], gslot[m % RING], coef[:, m:m + 1], acc[:, m % 2, :],
                                           ALU.mult, ALU.add).then_inc(S("g_used"), 1)
                    if parts:
                        spread_over(parts, m, ROUTE_ROWS[0])
                dve.wait_ge(S("g_used"), t * (2 * SLOTS) + 2 * SLOTS + RING)
                V.tensor_tensor(h2[:, bass.ds(t, 1), :].rearrange("p a b -> p (a b)"), acc[:, 0, :], acc[:, 1, :], ALU.add).then_inc(S("ex_ch"), 1)

            def experts(t, following):
                dve.wait_ge(S("g_used"), t * (2 * SLOTS) + RING)
                V.tensor_copy(hcur, h2[:, bass.ds(t, 1), :].rearrange("p a b -> p (a b)")).then_inc(S("ex_ch"), 1)
                dve.wait_ge(S("ex_ch"), t * 4 + 1)
                V.memset(acc, 0.0).then_inc(S("ex_ch"), 1)
                dve.wait_ge(S("ex_ch"), t * 4 + 2)
                parts = None if following is None else route(following, following + 1)
                for m in range(SLOTS):
                    row(t, 0, m)
                    dot(m, gslot[m % RING], hcur)
                    if parts:
                        spread_over(parts, m, ROUTE_ROWS[1])
                weigh_and_sum(t)

            dve.wait_ge(S("h2_ok"), 2 * NT)
            for m in range(SLOTS):
                dve.wait_ge(first_here[m % EARLY], (m // EARLY + 1) * 16)
                dve.wait_ge(S("g_used"), m + RING - 1)
                dot(m, gslot[RING - EARLY + m % EARLY], h2[:, 0, :])
            dve.wait_ge(S("q_mm"), 4 * EXPH)
            V.memset(acc[:, 0, :], 0.0).then_inc(S("ex_ch"), 1)
            V.memset(acc[:, 1, :], 0.0).then_inc(S("ex_ch"), 1)
            dve.wait_ge(S("sc_ok"), 4 * EXPH)
            weigh_and_sum(0, route(1, 2))
            with dve.Fori(1, NT - 1) as t:
                rown.offset, rown.passed = (t - 1) * per_route, S("dve_passed")
                experts(t, t + 1)
            experts(NT - 1, None)
            dve.wait_ge(S("ex_ch"), 4 * NT)
            own = Own(dve, S("fin_ch"))
            for t in range(NT):
                own.do(V.tensor_tensor(h2[:, t, :], h2[:, t, :], g2bc[:, min(t, 1), :], ALU.mult))
            own.settle()
            for t in range(NT):
                own.do(V.tensor_tensor(x[:, t, :], x[:, t, :], h2[:, t, :], ALU.add), S("x3_ok"))
            dve.wait_ge(S("fsq_ok"), NT)
            own.do(V.tensor_scalar(stat[:, 8:8 + NT], stat[:, 0:NT], 1.0 / D, EPS, ALU.mult, ALU.add), S("fms_ok"))
            dve.wait_ge(S("frt_ok"), 1)
            own.do(V.reciprocal(stat[:, 24:24 + NT], stat[:, 16:16 + NT]))
            own.settle()
            dve.wait_ge(S("ld_fn"), 16)
            for t in range(NT):
                own.do(V.scalar_tensor_tensor(x[:, t, :], x[:, t, :], stat[:, 24 + t:25 + t], fnorm, ALU.mult, ALU.mult), S("y_ok"))

        @block.gpsimd
        def _(pool):
            pool.wait_ge(S("lora_mm"), 3)
            pool.memset(sn, 0.0).then_inc(S("sn_zero"), 1)

            def take_ids(t, e):
                pool.wait_ge(S("eid_ok"), t + 1)
                pool.sem_inc(S("pool_passed"), 1)
                pool.tensor_copy(ibuf[e], eall[:, bass.ds(t, 1), :].rearrange("p a b -> p (a b)")).then_inc(S("ib_ok"), 1)
                pool.wait_ge(S("ib_ok"), t * 2 + e + 1)

            def gather(t, passes):
                for e in passes:
                    for m in range(SLOTS):
                        n = t * (2 * SLOTS) + e * SLOTS + m
                        pool.wait_ge(S("g_used"), n + 1)
                        if m == 0:
                            take_ids(t, e)
                        pool.sem_inc(S("pool_passed"), 1)
                        pool.indirect_dma_start(gslot[m % RING], None, a[("peer_u", "peer_v")[e]][0],
                                                bass.IndirectOffsetOnAxis(ap=ibuf[e][:, m:m + 1], axis=0)).then_inc(row_here[m % RING], 16)

            pool.wait_ge(S("q_mm"), 2 * EXPH + 4)
            take_ids(0, 0)
            for m in range(SLOTS):
                pool.wait_ge(S("g_used"), m + 1 + RING - EARLY)
                pool.indirect_dma_start(gslot[RING - EARLY + m % EARLY], None, a["peer_u"][0],
                                        bass.IndirectOffsetOnAxis(ap=ibuf[0][:, m:m + 1], axis=0)).then_inc(first_here[m % EARLY], 16)
            pool.wait_ge(S("q_mm"), 4 * EXPH)
            pool.wait_ge(S("sc_mm"), 4 * EXPH)
            gather(0, (1,))
            with pool.Fori(1, NT) as t:
                gather(t, (0, 1))



def small_rows(i):
    r = np.zeros((256, P), np.float32)
    r[0:48] = np.asarray(i["b_ada"])[0].reshape(48, P)
    r[48:56] = np.asarray(i["c_ctx"]).reshape(KD, P)
    r[56:64] = np.asarray(i["c"])[0].reshape(KD, P)
    r[64:72] = np.asarray(i["norm_mix"])[0].reshape(KD, P)
    r[72:80] = np.asarray(i["norm_ffn"])[0].reshape(KD, P)
    r[80, 0:64] = np.asarray(i["hy_f_b1"])[0]
    r[81, 0:64] = np.asarray(i["hy_f_b2"])[0]
    r[82:84, 0:64] = np.asarray(i["hy_freq"])[0]
    r[128:128 + 3 * NIN] = np.asarray(i["conv_w"])[0].reshape(3 * NIN, P)
    return r


OUTS = [(1, LC, D), (1, LL, D), (1, 1, 2, HEADS, HD, HD)]
RAW = ["x_prompt", "x_sample", "state_rwkv", "w_ada", "w_in", "w_out", "rwkv_w0", "rwkv_w1", "rwkv_w2", "rwkv_a0",
       "rwkv_a1", "rwkv_a2", "rwkv_g1", "rwkv_g2", "rwkv_k_k", "rwkv_k_a", "rwkv_r_k", "rwkv_ln_w", "rwkv_ln_b",
       "hy_f_w1", "hy_f_w2", "hy_f_w3", "hy_bias", "hy_norm", "peer_wq", "peer_keys", "peer_u", "peer_v", "final_norm"]


def layout(inputs):
    arrays = {n: np.ascontiguousarray(inputs[n]) for n in RAW}
    arrays["rows"] = small_rows(inputs)
    arrays["ident"] = np.eye(P, dtype=np.float32)
    i, j = np.arange(P)[:, None], np.arange(P)[None, :]
    same = i // CH == j // CH
    before = [same & (i < j), same & (i > j)]
    upto = [same & (i <= j), same & (i >= j)]
    arrays["tri"] = np.stack([np.stack([-SQD * upto[d], -SQD * before[d]], 1) for d in range(2)], 1).astype(np.float32)
    arrays["tot"] = (-SQD * (i // CH == np.arange(2)[None, :])).astype(np.float32)
    arrays["lmask"] = np.stack([np.stack([before[d], upto[d], before[1 - d]], 1) for d in range(2)], 1).astype(np.float32)
    for name, L in (("ctx", LC), ("lat", LL)):
        k, t = np.arange(L), np.arange(L)
        th = np.pi * ((2 * k[None, :] + 1) * t[:, None] % (4 * L)) / (2 * L)
        f = np.stack([np.cos(th), np.sin(th)])
        inv = np.transpose(f, (0, 2, 1)) / L
        for nm, m in (("f", f), ("i", inv)):
            m = m.reshape(2, L // P, P, L).transpose(2, 0, 1, 3).astype(np.float32)
            key = {"fctx": "fctx", "ictx": "ictx", "flat": "ftab", "ilat": "itab"}[nm + name]
            arrays[key] = np.ascontiguousarray(m[:, :, 0, :] if name == "ctx" else m)
    zs, ws = [], []
    for L in (LL, LC):
        t = np.linspace(0.0, 1.0, L, dtype=np.float32)[:, None]
        wpos = (2.0 * math.pi * np.arange(L, dtype=np.float32)[:, None] / L).astype(np.float32)
        f = np.linspace(1e-4, 7, 8, dtype=np.float32)[None, :]
        zs.append(np.concatenate([t, np.cos(f * wpos), -np.sin(f * wpos)], 1).T)
        deltas = np.linspace(math.log(1e-2) / 1.5, math.log(1e-2) / 0.3, DR, dtype=np.float32)
        ws.append(np.exp(-t * np.abs(deltas)))
    arrays["zT"] = np.ascontiguousarray(np.concatenate(zs, 1), np.float32)
    arrays["window"] = np.ascontiguousarray(np.concatenate([ws[1], ws[0]], 0).reshape(NT, P, DR).transpose(1, 0, 2), np.float32)
    arrays["iota16"] = np.tile(np.arange(TOPK, dtype=np.float32), (P, 1))
    arrays["i64"] = np.tile(np.eye(HD, dtype=np.float32), (2, 1))
    return arrays


def kernel(**inputs):
    import concourse.bacc as bacc
    from concourse.bass_utils import run_bass_kernel_spmd

    nc = bacc.Bacc("TRN2", target_bir_lowering=False, num_devices=1)
    arrays = layout(inputs)
    aps = {n: nc.dram_tensor(f"in_{n}", v.shape, mybir.dt.from_np(v.dtype), kind="ExternalInput").ap() for n, v in arrays.items()}
    outs = [nc.dram_tensor(f"out_{i}", shape, F32, kind="ExternalOutput").ap() for i, shape in enumerate(OUTS)]
    program(nc, aps, outs)
    r = run_bass_kernel_spmd(nc, [{f"in_{n}": v for n, v in arrays.items()}], core_ids=[0])
    return tuple(r.results[0][f"out_{i}"] for i in range(len(OUTS)))
```
